# Optimizing a Trainium2 kernel written in Bass

```python
import math
import jax
import jax.numpy as jnp
from jax import lax
import numpy as np

D_MODEL = 1024
BATCH = 1
SEQ = 512
DEPTH = 1
DEC_BATCH = 8
DEC_SEQ = 1
PAST_LEN = 2048
PAGE_SIZE = 128

N_META = 16
GLA_HEADS = 4
GLA_DK = 64
GLA_DV = 128
GLA_LOWRANK = 16
GLA_GATE_TAU = 16.0
GLA_CHUNK = 64
SWA_HEADS = 8
SWA_KV_HEADS = 2
SWA_HEAD_DIM = 64
SWA_GROUP = SWA_HEADS // SWA_KV_HEADS
WINDOW = 128
SWA_BLOCK = 128
NUM_BUCKETS = 32
MAX_DISTANCE = 128
N_EXPERTS = 32
TOP_K = 4
D_FF = 1024
SWIGLU_ALPHA = 1.702
SWIGLU_LIMIT = 7.0
MOE_BLOCK = 128
RMS_EPS = 1e-6

GLA_QK = GLA_HEADS * GLA_DK
GLA_V = GLA_HEADS * GLA_DV
SWA_Q = SWA_HEADS * SWA_HEAD_DIM
SWA_KV = SWA_KV_HEADS * SWA_HEAD_DIM
MIX_WIDTH = GLA_V + SWA_Q
IN_SIZES = (GLA_QK, GLA_QK, GLA_V, GLA_V, GLA_LOWRANK, SWA_Q, SWA_KV, SWA_KV)
D_IN = GLA_QK * 2 + GLA_V * 2 + GLA_LOWRANK + SWA_Q + SWA_KV * 2

kernel_name = "hymba_gla_swa_sink_moe_step"

def _split_points(sizes):
    pts, acc = [], 0
    for s in sizes[:-1]:
        acc += s
        pts.append(acc)
    return pts

def rms_norm(x, g):
    xf = x.astype(jnp.float32)
    y = xf * lax.rsqrt(jnp.mean(xf * xf, axis=-1, keepdims=True) + RMS_EPS)
    return (y * g.astype(jnp.float32)).astype(x.dtype)

def t5_bucket(dist):
    n = jnp.maximum(dist, 0)
    max_exact = NUM_BUCKETS // 2
    nf = jnp.maximum(n, 1).astype(jnp.float32)
    large = max_exact + (jnp.log(nf / max_exact) / math.log(MAX_DISTANCE / max_exact)
                         * (NUM_BUCKETS - max_exact)).astype(jnp.int32)
    large = jnp.minimum(large, NUM_BUCKETS - 1)
    return jnp.where(n < max_exact, n, large)

def project_mixer_inputs(h, w_in, w_a_up, b_a):
    lead = h.shape[:-1]
    gq, gk, gv, gr, ga, sq, sk, sv = jnp.split(h @ w_in, _split_points(IN_SIZES), axis=-1)
    gq = gq.reshape(*lead, GLA_HEADS, GLA_DK) * (GLA_DK ** -0.5)
    gk = gk.reshape(*lead, GLA_HEADS, GLA_DK)
    gv = gv.reshape(*lead, GLA_HEADS, GLA_DV)
    log_a = jax.nn.log_sigmoid((ga @ w_a_up + b_a).astype(jnp.float32)) / GLA_GATE_TAU
    log_a = log_a.reshape(*lead, GLA_HEADS, GLA_DK)
    sq = sq.reshape(*lead, SWA_KV_HEADS, SWA_GROUP, SWA_HEAD_DIM)
    sk = sk.reshape(*lead, SWA_KV_HEADS, SWA_HEAD_DIM)
    sv = sv.reshape(*lead, SWA_KV_HEADS, SWA_HEAD_DIM)
    return gq, gk, gv, gr, log_a, sq, sk, sv

def gla_chunked(q, k, v, log_a, s0, chunk):
    B, L, H, dk = q.shape
    dv = v.shape[-1]
    nc = L // chunk
    def to_chunks(t):
        return t.astype(jnp.float32).reshape(B, nc, chunk, H, t.shape[-1]).transpose(1, 0, 3, 2, 4)
    qc, kc, vc = to_chunks(q), to_chunks(k), to_chunks(v)
    bc = jnp.cumsum(to_chunks(log_a), axis=-2)
    causal = jnp.tril(jnp.ones((chunk, chunk), jnp.float32))

    def step(S, inp):
        qi, ki, vi, bi = inp
        qt = qi * jnp.exp(bi)
        kt = ki * jnp.exp(-bi)
        A = jnp.einsum('bhtd,bhsd->bhts', qt, kt) * causal
        o = jnp.einsum('bhtd,bhde->bhte', qt, S) + jnp.einsum('bhts,bhse->bhte', A, vi)
        b_last = bi[..., -1:, :]
        S = jnp.exp(b_last[..., 0, :])[..., :, None] * S + jnp.einsum(
            'bhsd,bhse->bhde', ki * jnp.exp(b_last - bi), vi)
        return S, o

    S, o = lax.scan(step, s0.astype(jnp.float32), (qc, kc, vc, bc))
    o = o.transpose(1, 0, 3, 2, 4).reshape(B, L, H, dv)
    return o, S

def sink_attention(q, k, v, dist, valid, sinks, bias_table):
    s = jnp.einsum('...qhgd,...shd->...hgqs', q, k).astype(jnp.float32) * (SWA_HEAD_DIM ** -0.5)
    Qn, Kn = dist.shape
    bias = bias_table.astype(jnp.float32)[t5_bucket(dist)]
    bias = jnp.moveaxis(bias, -1, 0).reshape(SWA_KV_HEADS, SWA_GROUP, Qn, Kn)
    s = jnp.where(valid, s + bias, -jnp.inf)
    sink = sinks.astype(jnp.float32).reshape(SWA_KV_HEADS, SWA_GROUP, 1, 1)
    m = jnp.maximum(jnp.max(s, axis=-1, keepdims=True), sink)
    p = jnp.exp(s - m)
    p = p / (jnp.sum(p, axis=-1, keepdims=True) + jnp.exp(sink - m))
    return jnp.einsum('...hgqs,...shd->...qhgd', p.astype(v.dtype), v)

def swa_prompt(q, k, v, sinks, bias_table):
    B, L = q.shape[:2]
    nb = -(-L // SWA_BLOCK)
    pad = nb * SWA_BLOCK - L
    def pad_end(t):
        return jnp.pad(t, [(0, 0), (0, pad)] + [(0, 0)] * (t.ndim - 2))
    qb = pad_end(q).reshape(B, nb, SWA_BLOCK, SWA_KV_HEADS, SWA_GROUP, SWA_HEAD_DIM)
    kb = pad_end(k).reshape(B, nb, SWA_BLOCK, SWA_KV_HEADS, SWA_HEAD_DIM)
    vb = pad_end(v).reshape(B, nb, SWA_BLOCK, SWA_KV_HEADS, SWA_HEAD_DIM)
    def with_prev(t):
        prev = jnp.pad(t, [(0, 0), (1, 0), (0, 0), (0, 0), (0, 0)])[:, :-1]
        return jnp.concatenate([prev, t], axis=2)
    i = jnp.arange(SWA_BLOCK)[:, None]
    j = jnp.arange(2 * SWA_BLOCK)[None, :]
    dist = i - j + SWA_BLOCK
    blk = jnp.arange(nb)[:, None, None]
    key_exists = (blk * SWA_BLOCK - SWA_BLOCK + j[None]) >= 0
    valid = ((dist >= 0) & (dist < WINDOW))[None] & key_exists
    o = sink_attention(qb, with_prev(kb), with_prev(vb), dist, valid[:, None, None], sinks, bias_table)
    return o.reshape(B, nb * SWA_BLOCK, SWA_HEADS, SWA_HEAD_DIM)[:, :L]

def swa_sample(q, k, v, cache_k, cache_v, sinks, bias_table):
    S = q.shape[1]
    kk = jnp.concatenate([cache_k.astype(k.dtype), k], axis=1)
    vv = jnp.concatenate([cache_v.astype(v.dtype), v], axis=1)
    i = jnp.arange(S)[:, None]
    j = jnp.arange(WINDOW + S)[None, :]
    dist = i + WINDOW - j
    valid = (dist >= 0) & (dist < WINDOW)
    o = sink_attention(q, kk, vv, dist, valid, sinks, bias_table)
    return o.reshape(q.shape[0], S, SWA_HEADS, SWA_HEAD_DIM), kk[:, -WINDOW:], vv[:, -WINDOW:]

def combine_mixer_outputs(o_gla, gr, o_swa, g_gla_out, g_swa_out, w_out, dtype):
    lead = o_gla.shape[:-2]
    gate = jax.nn.silu(gr.astype(jnp.float32)).reshape(*lead, GLA_HEADS, GLA_DV)
    o_gla = (rms_norm(o_gla, g_gla_out) * gate).reshape(*lead, GLA_V)
    o_swa = rms_norm(o_swa.reshape(*lead, SWA_Q), g_swa_out)
    o = jnp.concatenate([o_gla.astype(dtype), o_swa.astype(dtype)], axis=-1)
    return o @ w_out

def mixer_prompt(h, mp, bias_table):
    w_in, w_a_up, b_a, g_gla_out, g_swa_out, sinks, w_out = mp
    gq, gk, gv, gr, log_a, sq, sk, sv = project_mixer_inputs(h, w_in, w_a_up, b_a)
    B, L = h.shape[:2]
    pad = (-L) % GLA_CHUNK
    def pad_front(t):
        return jnp.pad(t, [(0, 0), (pad, 0), (0, 0), (0, 0)])
    s0 = jnp.zeros((B, GLA_HEADS, GLA_DK, GLA_DV), jnp.float32)
    o_gla, s_new = gla_chunked(pad_front(gq), pad_front(gk), pad_front(gv), pad_front(log_a), s0, GLA_CHUNK)
    o_gla = o_gla[:, pad:]
    o_swa = swa_prompt(sq, sk, sv, sinks, bias_table)
    out = combine_mixer_outputs(o_gla, gr, o_swa, g_gla_out, g_swa_out, w_out, h.dtype)
    return out, s_new, sk[:, -WINDOW:], sv[:, -WINDOW:]

def mixer_sample(h, s0, cache_k, cache_v, mp, bias_table):
    w_in, w_a_up, b_a, g_gla_out, g_swa_out, sinks, w_out = mp
    gq, gk, gv, gr, log_a, sq, sk, sv = project_mixer_inputs(h, w_in, w_a_up, b_a)
    o_gla, s_new = gla_chunked(gq, gk, gv, log_a, s0, h.shape[1])
    o_swa, k_new, v_new = swa_sample(sq, sk, sv, cache_k, cache_v, sinks, bias_table)
    out = combine_mixer_outputs(o_gla, gr, o_swa, g_gla_out, g_swa_out, w_out, h.dtype)
    return out, s_new, k_new, v_new

def clamped_swiglu(hh):
    gate = jnp.minimum(hh[..., :D_FF], SWIGLU_LIMIT)
    lin = jnp.clip(hh[..., D_FF:], -SWIGLU_LIMIT, SWIGLU_LIMIT)
    return gate * jax.nn.sigmoid(SWIGLU_ALPHA * gate) * (lin + 1)

def moe_ffn(x2d, w_router, b_router, w_up, b_up, w_down, b_down):
    T, D = x2d.shape
    logits = (x2d @ w_router).astype(jnp.float32) + b_router.astype(jnp.float32)
    top_v, top_e = lax.top_k(logits, TOP_K)
    gates = jax.nn.softmax(top_v, axis=-1)
    n_slots = T * TOP_K
    slot_e = top_e.reshape(-1)
    slot_tok = jnp.repeat(jnp.arange(T, dtype=jnp.int32), TOP_K)
    slot_g = gates.reshape(-1)
    order = jnp.argsort(slot_e)
    e_sorted = slot_e[order]
    counts = jnp.bincount(slot_e, length=N_EXPERTS)
    padded = (counts + MOE_BLOCK - 1) // MOE_BLOCK * MOE_BLOCK
    pad_end = jnp.cumsum(padded)
    pad_start = pad_end - padded
    start = jnp.cumsum(counts) - counts
    dest = pad_start[e_sorted] + jnp.arange(n_slots) - start[e_sorted]
    n_blocks = -(-n_slots // MOE_BLOCK) + N_EXPERTS
    n_pad = n_blocks * MOE_BLOCK
    tok_of_slot = jnp.full((n_pad,), T, jnp.int32).at[dest].set(slot_tok[order])
    g_of_slot = jnp.zeros((n_pad,), jnp.float32).at[dest].set(slot_g[order])
    blk_e = jnp.minimum(jnp.searchsorted(pad_end, jnp.arange(n_blocks) * MOE_BLOCK, side='right'),
                        N_EXPERTS - 1)
    xs = jnp.concatenate([x2d, jnp.zeros((1, D), x2d.dtype)], axis=0)[tok_of_slot]
    xs = xs.reshape(n_blocks, MOE_BLOCK, D)

    def expert_block(args):
        xb, e = args
        hh = xb @ w_up[e] + b_up[e]
        return clamped_swiglu(hh) @ w_down[e] + b_down[e]

    ys = lax.map(expert_block, (xs, blk_e)).reshape(n_pad, D)
    ys = ys * g_of_slot[:, None].astype(ys.dtype)
    return jnp.zeros((T + 1, D), ys.dtype).at[tok_of_slot].add(ys)[:T]

def setup_inputs(seed: int = 0) -> dict:
    key = jax.random.key(seed)
    ks = iter(jax.random.split(key, 32))
    f32 = jnp.float32
    def nrm(shape, scale=1.0):
        return jax.random.normal(next(ks), shape, f32) * scale
    def gain(shape):
        return 1.0 + nrm(shape, 0.1)
    return {
        "x_prompt": nrm((BATCH, SEQ, D_MODEL)),
        "x_sample": nrm((DEC_BATCH, DEC_SEQ, D_MODEL)),
        "state_gla": nrm((DEPTH, DEC_BATCH, GLA_HEADS, GLA_DK, GLA_DV)),
        "cache_swa_k": nrm((DEPTH, DEC_BATCH, WINDOW, SWA_KV_HEADS, SWA_HEAD_DIM)),
        "cache_swa_v": nrm((DEPTH, DEC_BATCH, WINDOW, SWA_KV_HEADS, SWA_HEAD_DIM)),
        "meta_tokens": nrm((N_META, D_MODEL)),
        "rel_bias_table": nrm((NUM_BUCKETS, SWA_HEADS), 0.5),
        "g_mix": gain((DEPTH, D_MODEL)),
        "w_in": nrm((DEPTH, D_MODEL, D_IN), D_MODEL ** -0.5),
        "w_a_up": nrm((DEPTH, GLA_LOWRANK, GLA_QK), GLA_LOWRANK ** -0.5),
        "b_a": nrm((DEPTH, GLA_QK), 0.1),
        "g_gla_out": gain((DEPTH, GLA_DV)),
        "g_swa_out": gain((DEPTH, SWA_Q)),
        "attn_sinks": nrm((DEPTH, SWA_HEADS), 0.5),
        "w_out": nrm((DEPTH, MIX_WIDTH, D_MODEL), MIX_WIDTH ** -0.5),
        "g_ffn": gain((DEPTH, D_MODEL)),
        "w_router": nrm((DEPTH, D_MODEL, N_EXPERTS), D_MODEL ** -0.5),
        "b_router": nrm((DEPTH, N_EXPERTS), 0.01),
        "w_up": nrm((DEPTH, N_EXPERTS, D_MODEL, 2 * D_FF), D_MODEL ** -0.5),
        "b_up": nrm((DEPTH, N_EXPERTS, 2 * D_FF), 0.01),
        "w_down": nrm((DEPTH, N_EXPERTS, D_FF, D_MODEL), D_FF ** -0.5),
        "b_down": nrm((DEPTH, N_EXPERTS, D_MODEL), 0.01),
        "g_final": gain((D_MODEL,)),
    }

def reference(x_prompt, x_sample, state_gla, cache_swa_k, cache_swa_v, meta_tokens, rel_bias_table,
              g_mix, w_in, w_a_up, b_a, g_gla_out, g_swa_out, attn_sinks, w_out,
              g_ffn, w_router, b_router, w_up, b_up, w_down, b_down, g_final):
    B = x_prompt.shape[0]
    meta = jnp.broadcast_to(meta_tokens.astype(x_prompt.dtype)[None], (B, N_META, D_MODEL))
    xp = jnp.concatenate([meta, x_prompt], axis=1)
    xs = x_sample
    sp_list, kp_list, vp_list, ss_list, ks_list, vs_list = [], [], [], [], [], []
    for l in range(DEPTH):
        mp = (w_in[l], w_a_up[l], b_a[l], g_gla_out[l], g_swa_out[l], attn_sinks[l], w_out[l])
        mix_p, s_p, k_p, v_p = mixer_prompt(rms_norm(xp, g_mix[l]), mp, rel_bias_table)
        mix_s, s_s, k_s, v_s = mixer_sample(rms_norm(xs, g_mix[l]), state_gla[l], cache_swa_k[l],
                                            cache_swa_v[l], mp, rel_bias_table)
        xp = xp + mix_p
        xs = xs + mix_s
        if l == DEPTH - 1:
            xp = xp[:, N_META:]
        hp = rms_norm(xp, g_ffn[l])
        hs = rms_norm(xs, g_ffn[l])
        xp = xp + moe_ffn(hp.reshape(-1, D_MODEL), w_router[l], b_router[l], w_up[l], b_up[l],
                          w_down[l], b_down[l]).reshape(xp.shape)
        xs = xs + moe_ffn(hs.reshape(-1, D_MODEL), w_router[l], b_router[l], w_up[l], b_up[l],
                          w_down[l], b_down[l]).reshape(xs.shape)
        sp_list.append(s_p)
        kp_list.append(k_p)
        vp_list.append(v_p)
        ss_list.append(s_s)
        ks_list.append(k_s)
        vs_list.append(v_s)
    y_prompt = rms_norm(xp, g_final)
    y_sample = rms_norm(xs, g_final)
    new_state_gla_prompt = jnp.stack(sp_list)
    new_cache_swa_k_prompt = jnp.stack(kp_list)
    new_cache_swa_v_prompt = jnp.stack(vp_list)
    new_state_gla_sample = jnp.stack(ss_list)
    new_cache_swa_k_sample = jnp.stack(ks_list)
    new_cache_swa_v_sample = jnp.stack(vs_list)
    return (y_prompt, y_sample, new_state_gla_prompt, new_cache_swa_k_prompt, new_cache_swa_v_prompt,
            new_state_gla_sample, new_cache_swa_k_sample, new_cache_swa_v_sample)


_drawn_inputs = setup_inputs


def setup_inputs(seed=0):
    import zlib

    import numpy as np

    out = dict(_drawn_inputs(seed))
    spreads = {}
    factors = {'attn_sinks': 8.0, 'b_up': 8.0, 'b_down': 8.0}
    for name, (base, spread) in spreads.items():
        noise = np.random.default_rng([zlib.crc32(name.encode()), seed]).standard_normal(out[name].shape)
        drawn = base * np.exp(spread * noise) if base else spread * noise
        out[name] = jnp.asarray(drawn.astype(out[name].dtype))
    for name, factor in factors.items():
        out[name] = (out[name] * factor).astype(out[name].dtype)
    return out
```

```python
import math
from contextlib import ExitStack

import concourse.bass as bass
from concourse import mybir

F32 = mybir.dt.float32
F32R = mybir.dt.float32r
BF16 = mybir.dt.bfloat16
I32 = mybir.dt.int32
U32 = mybir.dt.uint32
ALU = mybir.AluOpType
ACT = mybir.ActivationFunctionType
AX = mybir.AxisListType.X

P = 128
D = 1024
KT = D // P
SEQ, META, NS = 512, 16, 8
SMALL = META + NS
PT = SEQ // P
NTILE = PT + 1
T = SMALL + SEQ
HALF = T // 2
TOK = SEQ + NS
GH, DK, DV, LOWRANK, CHUNK = 4, 64, 128, 16, 64
QH, KVH, HD, WIN = 8, 2, 64, 128
NE, TOPK, FF = 32, 4, 1024
ALPHA, LIMIT, EPS, TAU = 1.702, 7.0, 1e-6, 16.0
BUCKETS = 32
GQ, GK, GV = 0, GH * DK, 2 * GH * DK
GR = GV + GH * DV
GA = GR + GH * DV
SQ = GA + LOWRANK
SK = SQ + QH * HD
SV = SK + KVH * HD
DIN = SV + KVH * HD
MASKED = -1e30
MAXBLK = NE + TOK * TOPK // P
BLKS = MAXBLK + 2
FAR = 65536.0
UNIT = 2048
UPU, DNU, RING = 8, 4, 4
UPB = UPU + DNU
SQRT_HD = HD ** -0.5


def moe_layer(nc, x_prompt, x_sample, state_gla, cache_k, cache_v, meta, bias_tab, g_mix, w_in, w_a_up, b_a,
              g_gla, g_swa, sinks, w_out, g_ffn, w_router, b_router, w_up, b_up, w_down, b_down, g_final,
              bucket_hot, y_p, y_s, st_p, ck_p, cv_p, st_s, ck_s, cv_s):
    xn_dram = nc.dram_tensor("expert_inputs", (TOK, D), F32, kind="Internal").ap()
    x2_dram = nc.dram_tensor("residual", (TOK, D), F32, kind="Internal").ap()
    slot_dram = nc.dram_tensor("slot_outputs", (TOK * TOPK, D), F32, kind="Internal").ap()
    skew_dram = nc.dram_tensor("bias_rows", (P, QH * 3 * P), F32, kind="Internal").ap()

    rows = [SMALL] + [P] * PT
    cols = [(0, SMALL)] + [(SMALL + P * i, SMALL + P * (i + 1)) for i in range(PT)]

    with ExitStack() as ctx:
        def sem(name):
            return ctx.enter_context(nc.semaphore(name))

        base = (nc.sbuf_base + 31) // 32 * 32
        room = (nc.sbuf_usable_end - base) // 32 * 32
        ctx.enter_context(nc.sbuf_tensor("arena", [P, (room - 64) // 4], F32))

        class Region:

            def __init__(self, start, end):
                self.at, self.end = start, end

            def __call__(self, name, shape, dt=F32):
                n = math.prod(shape[1:]) * (2 if dt == BF16 else 4)
                t = nc.alloc_sbuf_tensor_at(name, list(shape), dt, offset=base + self.at)
                self.at += (n + 31) // 32 * 32
                assert self.at <= self.end, (name, self.at, self.end)
                return t

        RAW0, SPL0 = 0, UPB * UNIT * 4
        WORK0 = SPL0 + 2 * RING * UNIT * 4
        KEEP0 = WORK0 + 9 * D * 4
        END = room - 64

        keep = Region(KEEP0, END)
        ident = keep("ident", [P, P])
        slots_row = keep("slots_row", [P, P])
        bias_parts = keep("bias_parts", [P, 3 * D], BF16)
        pos_table = keep("pos_table", [P, NTILE, NE])
        slot_table = keep("slot_table", [P, NTILE, NE, 4], BF16)
        gates = keep("gates", [P, NTILE, TOPK])
        blk_expert = keep("blk_expert", [P, BLKS])
        blk_start = keep("blk_start", [P, BLKS])
        blk_row = keep("blk_row", [1, BLKS + 1], I32)
        expert_of_row = keep("expert_of_row", [P, 1])
        hit = keep("hit", [P, NTILE, P], BF16)
        sel_up = keep("sel_up", [P, P], BF16)
        sel_dn = keep("sel_dn", [P, P], BF16)
        shifted = keep("shifted", [P, NTILE])
        slot_cols = keep("slot_cols", [P, NTILE, 4], BF16)
        found = keep("found", [P, 4])
        empty = keep("empty", [P, 1])
        token_f = keep("token_f", [P, 1])
        slot_f = keep("slot_f", [P, 1])
        token_idx = keep("token_idx", [P, 1], I32)
        slot_idx = keep("slot_idx", [P, 4], I32)
        slot_tmp = keep("slot_tmp", [P, 3], I32)

        R = Region(RAW0, SPL0)
        raw = R("raw", [P, UPB, UNIT])
        R = Region(SPL0, WORK0)
        w_hi = R("w_hi", [P, RING, UNIT], F32R)
        w_lo = R("w_lo", [P, RING, UNIT], F32R)
        R = Region(WORK0, KEEP0)
        x_rows = R("x_rows", [P, D])
        xT_hi = R("xT_hi", [P, KT, P], F32R)
        xT_lo = R("xT_lo", [P, KT, P], F32R)
        aT_hi = R("aT_hi", [P, KT, P], F32R)
        aT_lo = R("aT_lo", [P, KT, P], F32R)
        act_g = R("act_g", [P, D])
        act_s = R("act_s", [P, D])
        act_l = R("act_l", [P, D])
        y_rows = R("y_rows", [P, D])
        R = Region(RAW0, SPL0)
        t_slots = [R(f"t_slots{i}", [P, TOPK, D]) for i in range(3)]
        t_x2 = [R(f"t_x2{i}", [P, D]) for i in range(3)]
        t_sq = R("t_sq", [P, D])
        g_final_bc = R("g_final_bc", [P, D])
        R = Region(SPL0, WORK0)
        t_stat = R("t_stat", [P, NTILE, 4])

        R = Region(RAW0, SPL0)
        w_in_sb = R("w_in_sb", [P, KT, DIN])
        x_sb = R("x_sb", [P, NTILE, D])
        R = Region(SPL0, KEEP0)
        hT = R("hT", [P, KT, T])
        sqT = R("sqT", [P, 4, T])
        skT = R("skT", [P, T])
        gla0 = R.at
        gqT = R("gqT", [P, 2, T])
        gkT = R("gkT", [P, 2, T])
        decay = R("decay", [P, 2, T])
        e_pos = R("e_pos", [P, 2, T])
        qd = R("qd", [P, 2, T])
        kd = R("kd", [P, 2, T])
        ks = R("ks", [P, 2, T])
        B = Region(gla0, R.at)
        b_stage = B("b_stage", [3 * NE, 3 * D])
        B = Region(gla0 + 3 * 2 * T * 4, R.at)
        skew_src = B("skew_src", [P, QH, 3 * P])
        ks_rows = R("ks_rows", [P, NTILE, 2, P])
        gv = R("gv", [P, NTILE, GH * DV])
        gate = R("gate", [P, NTILE, GH * DV])
        sv = R("sv", [P, NTILE, KVH * HD])
        states = R("states", [P, NS, 2, DV])
        w_a_sb = R("w_a_sb", [LOWRANK, GH * DK])
        gaT = R("gaT", [LOWRANK, T])
        m_keep = R("m_keep", [P, NTILE, NE], BF16)
        g_mixT = R("g_mixT", [P, KT])
        g_outT = R("g_outT", [P, KT])
        b_aT = R("b_aT", [P, 2])
        b_rT = R("b_rT", [NE, 1])
        stat = R("stat", [P, 16])
        sink_bc = R("sink_bc", [P, QH])
        sink_col = R("sink_col", [QH, 1])
        row_ok = R("row_ok", [SMALL, 1])
        pidx = R("pidx", [P, 1])
        before = R("before", [P, P], BF16)
        ones_b = R("ones_b", [P, P], BF16)
        ones_f = R("ones_f", [16, P])
        same_chunk = R("same_chunk", [P, P])
        tab_sb = R("tab_sb", [BUCKETS, QH])
        hot_sb = R("hot_sb", [BUCKETS, WIN])
        bias_s = R("bias_s", [QH, WIN])
        norm = R("norm", [P, 48])
        soft = R("soft", [P, 4, QH])
        top_v = R("top_v", [P, 8])
        top_i = R("top_i", [P, 8], U32)
        top_f = R("top_f", [P, 8])
        pT_s = R("pT_s", [P, NS, QH])
        small_s = R("small_s", [QH, 4, NS])
        B = Region(SPL0, SPL0 + KT * T * 4)
        gla_state = B("gla_state", [P, 9, 2, DV])
        q_diag = B("q_diag", [P, 2, NS, SMALL])
        q_swa = B("q_swa", [P, NS, QH])
        a_gla = B("a_gla", [P, GH, P])
        lgT = B("lgT", [NE, P])
        EARLY = 1
        B = Region(RAW0 + EARLY * UNIT * 4, SPL0)
        w_out_sb = B("w_out_sb", [P, KT, D])
        bias_sb = B("bias_sb", [P, QH, 2 * P])
        probs_at = B.at
        probs = B("probs", [P, QH, 2 * P])
        pT_at = B.at
        pT = B("pT", [P, 4, 4, P])
        mix = B("mix", [P, D])
        mixT = B("mixT", [P, KT, P])
        h2_at = B.at
        h2 = B("h2", [P, D])
        g_ffn_bc = B("g_ffn_bc", [P, D])
        w_router_sb = B("w_router_sb", [P, KT, NE])
        xr = B("xr", [P, D])
        sample_at = B.at
        k_s = B("k_s", [P, NS, KVH * HD])
        v_s = B("v_s", [P, NS, KVH * HD])
        k_rows_s = B("k_rows_s", [SMALL, 2, P])
        sk_rows_s = B("sk_rows_s", [SMALL, P])
        ck_rows = B("ck_rows", [P, P])
        k_diag = Region(probs_at, pT_at)("k_diag", [SMALL, NS, 2 * P])
        B = Region(pT_at, pT_at + 2 * D * 4)
        p_s = B("p_s", [QH, NS, WIN])
        kT_s = B("kT_s", [P, NS, P])
        B = Region(h2_at, h2_at + D * 4)
        o_s = B("o_s", [QH, NS, P])
        B = Region(sample_at, sample_at + D * 4)
        one_hot = B("one_hot", [P, TOPK, NE])
        one_hot_k = B("one_hot_k", [P, TOPK, NE])
        over = B("over", [P, 4, NE])
        over_end = B("over_end", [P, 4, NE])
        zT = nc.alloc_sbuf_tensor_at("zT", [P, 2, T], F32, offset=base + gla0 + 6 * 2 * T * 4)
        z_l = nc.alloc_sbuf_tensor_at("z_l", [P, 2, T], F32, offset=base + gla0 + 3 * 2 * T * 4)
        scan_keep = nc.alloc_sbuf_tensor_at("scan_keep", [P, T], F32, offset=base + gla0 + 4 * 2 * T * 4)
        ps = ctx.enter_context(nc.psum_tensor("ps", [P, 8, 512], F32))

        ld_x = [sem(f"ld_x{t}") for t in range(NTILE)]
        ld_win = [sem(f"ld_win{k}") for k in range(KT)]
        ld_tables, ld_small, ld_biases = sem("ld_tables"), sem("ld_small"), sem("ld_biases")
        ld_wout, ld_sample, ld_new_rows, ld_attn = sem("ld_wout"), sem("ld_sample"), sem("ld_new_rows"), sem("ld_attn")
        ld_xr, skew_written, skew_read, o_moved = sem("ld_xr"), sem("skew_written"), sem("skew_read"), sem("o_moved")
        outputs = sem("outputs")
        consts, flanks, parts_made, scan_set = sem("consts"), sem("flanks"), sem("parts_made"), sem("scan_set")
        x_var, x_root, x_rstd, hn_ready = sem("x_var"), sem("x_root"), sem("x_rstd"), sem("hn_ready")
        hT_psum, hT_ready = sem("hT_psum"), sem("hT_ready")
        skew_psum, skew_filled, scan_cleared = sem("skew_psum"), sem("skew_filled"), sem("scan_cleared")
        colp_psum, colp_copied = sem("colp_psum"), sem("colp_copied")
        rowp_psum, gv_copied, sig_made, sv_copied, gate_made = (
            sem("rowp_psum"), sem("gv_copied"), sem("sig_made"), sem("sv_copied"), sem("gate_made"))
        soft_ready, decay_ready, exps_ready, gla_ready = sem("soft_ready"), sem("decay_ready"), sem("exps_ready"), sem("gla_ready")
        rowsT_psum, rowsT_copied, kv_psum, state_made = sem("rowsT_psum"), sem("rowsT_copied"), sem("kv_psum"), sem("state_made")
        a_psum, a_masked, o_psum, o_copied = sem("a_psum"), sem("a_masked"), sem("o_psum"), sem("o_copied")
        diags_made, outer_psum, s_state_made = sem("diags_made"), sem("outer_psum"), sem("s_state_made")
        ksT_psum, ksT_copied, s_score_psum, s_shifted, s_exp, s_probs = (
            sem("ksT_psum"), sem("ksT_copied"), sem("s_score_psum"), sem("s_shifted"), sem("s_exp"), sem("s_probs"))
        s_pT_psum, s_pT_copied, s_pv_psum, s_o_copied = sem("s_pT_psum"), sem("s_pT_copied"), sem("s_pv_psum"), sem("s_o_copied")
        score_psum, max_ready, exp_done, pT_psum, pT_copied, pv_psum, pv_copied = (
            sem("score_psum"), sem("max_ready"), sem("exp_done"), sem("pT_psum"), sem("pT_copied"), sem("pv_psum"), sem("pv_copied"))
        m_var, m_root, mix_ready, mixT_psum, mixT_ready, out_psum, x2_ready = (
            sem("m_var"), sem("m_root"), sem("mix_ready"), sem("mixT_psum"), sem("mixT_ready"), sem("out_psum"), sem("x2_ready"))
        x2_var, x2_root, h2_ready, h2_stored, x2_stored = sem("x2_var"), sem("x2_root"), sem("h2_ready"), sem("h2_stored"), sem("x2_stored")
        h2T_psum, h2T_ready, lgT_psum, lgT_ready, lg_psum, top_ready, gate_exp, routed = (
            sem("h2T_psum"), sem("h2T_ready"), sem("lgT_psum"), sem("lgT_ready"), sem("lg_psum"), sem("top_ready"), sem("gate_exp"), sem("routed"))
        pos_psum, over_made, over_psum, table_made = sem("pos_psum"), sem("over_made"), sem("over_psum"), sem("table_made")
        mixer_left = sem("mixer_left")
        rows_asked = sem("rows_asked")
        landed = [sem(f"landed{j}") for j in range(UPB)]
        slot_used = sem("slot_used")
        hi_ready, lo_ready = sem("hi_ready"), sem("lo_ready")
        hit_ready, list_psum, idx_ready, gathered = sem("hit_ready"), sem("list_psum"), sem("idx_ready"), sem("gathered")
        aged = sem("aged")
        xT_psum, xT_hi_ready, xT_ready = sem("xT_psum"), sem("xT_hi_ready"), sem("xT_ready")
        sel_up_ready, sel_dn_ready, up_bias_done, dn_bias_done = (
            sem("sel_up_ready"), sem("sel_dn_ready"), sem("up_bias_done"), sem("dn_bias_done"))
        up_read, g_ready, sigm_ready, a_ready = sem("up_read"), sem("g_ready"), sem("sigm_ready"), sem("a_ready")
        aT_psum, aT_hi_ready, aT_ready = sem("aT_psum"), sem("aT_hi_ready"), sem("aT_ready")
        y_ready, scattered = sem("y_ready"), sem("scattered")
        t_loaded = [sem(f"t_loaded{i}") for i in range(3)]
        ld_gfinal, t_var, t_root, t_y, t_zero = sem("ld_gfinal"), sem("t_var"), sem("t_root"), sem("t_y"), sem("t_zero")
        t_stored = [sem(f"t_stored{i}") for i in range(3)]
        dve_own, act_own, pool_own = sem("dve_own"), sem("act_own"), sem("pool_own")

        def bc(ap, axis, shape):
            return ap.unsqueeze(axis).to_broadcast(list(shape))

        def head(h):
            return slice(DK * (h % 2), DK * (h % 2) + DK), h // 2

        COLP = ([("ga", GA, LOWRANK), ("gk0", GK, P), ("gk1", GK + P, P), ("gq0", GQ, P), ("gq1", GQ + P, P),
                 ("z0", 0, P), ("z1", P, P), ("sk", SK, P)] + [(f"sq{j}", SQ + j * P, P) for j in range(4)])
        NCOLP = 2 * len(COLP)
        NZ = 14

        class Own:

            def __init__(self, eng, s, start=0):
                self.eng, self.s, self.start, self.n = eng, s, start, 0

            def step(self, ins):
                ins.then_inc(self.s, 1)
                self.n += 1
                return ins

            def settle(self):
                self.eng.wait_ge(self.s, self.start + self.n)

            def do(self, ins):
                self.step(ins)
                self.settle()

        NCONST = 16 + 2 * NTILE
        NB_ROW = blk_row[0:1, BLKS:BLKS + 1]



        def up_end(b):
            return UPB if isinstance(b, int) and b == 0 else UPB * b + UPU

        def block_count(e):
            return e.value_load(NB_ROW, min_val=NE - 2, max_val=MAXBLK - 2) + 2

        def expert(e, b):
            if isinstance(b, int):
                return b
            return e.value_load(blk_row[0:1, bass.ds(b, 1)], min_val=0, max_val=NE - 1)

        block = ctx.enter_context(nc.Block())

        @block.gpsimd
        def _(pool):
            own = Own(pool, pool_own)
            made = Own(pool, consts)
            pool.memset(ident[:], 0.0).then_inc(pool_own, 1)
            pool.memset(same_chunk[:], 1.0).then_inc(pool_own, 1)
            pool.memset(before[:], 1.0).then_inc(pool_own, 1)
            pool.memset(row_ok[:], 1.0).then_inc(pool_own, 1)
            own.n = 4
            own.settle()
            made.do(pool.affine_select(out=ident[:], in_=ident[:], compare_op=ALU.not_equal, fill=1.0, base=0,
                               pattern=[[-1, P]], channel_multiplier=1))
            pool.memset(skew_src[:, :, 0:P], MASKED).then_inc(flanks, 1)
            pool.memset(skew_src[:, :, 2 * P:3 * P], MASKED).then_inc(flanks, 1)
            made.do(pool.affine_select(out=before[:], in_=before[:], compare_op=ALU.is_gt, fill=0.0, base=0,
                               pattern=[[1, P]], channel_multiplier=-1))
            own.do(pool.affine_select(out=same_chunk[:], in_=same_chunk[:], compare_op=ALU.is_ge, fill=0.0, base=0,
                                      pattern=[[1, P]], channel_multiplier=-1))
            made.do(pool.memset(same_chunk[0:CHUNK, CHUNK:P], 0.0))
            made.do(pool.affine_select(out=row_ok[:], in_=row_ok[:], compare_op=ALU.is_ge, fill=0.0, base=-META,
                               pattern=[[0, 1]], channel_multiplier=1))
            made.do(pool.memset(ones_b[:], 1.0))
            made.do(pool.memset(ones_f[:], 1.0))
            made.do(pool.iota(slots_row[:], pattern=[[1, P]], base=0, channel_multiplier=0,
                      allow_small_or_imprecise_dtypes=True))
            made.do(pool.iota(pidx[:], pattern=[[0, 1]], base=0, channel_multiplier=1,
                      allow_small_or_imprecise_dtypes=True))
            for j in range(3):
                made.do(pool.iota(expert_of_row[NE * j:NE * j + NE, :], pattern=[[0, 1]], base=0, channel_multiplier=1,
                          allow_small_or_imprecise_dtypes=True))
            made.do(pool.memset(expert_of_row[3 * NE:P, :], -1.0))
            made.do(pool.memset(m_keep[:], 0.0))
            assert made.n == NCONST - 2 * NTILE - 3
            for t in range(NTILE):
                first = SEQ - META if t == 0 else P * (t - 1)
                made.do(pool.iota(slot_table[:, t, :, 0], pattern=[[0, NE]], base=0, channel_multiplier=1,
                          allow_small_or_imprecise_dtypes=True))
                made.do(pool.memset(slot_table[:, t, :, 1], first / 16.0))
            made.do(pool.memset(slot_table[:, :, :, 2], 0.0))
            made.do(pool.memset(slot_table[:, :, :, 3], 1.0))
            made.do(pool.memset(gates[:], 0.0))
            pool.wait_ge(ld_biases, 6 * 16)
            own.do(pool.memset(bias_parts[:], 0.0))
            own.do(pool.tensor_copy(bias_parts[0:3 * NE, :], b_stage[:]))
            own.do(pool.tensor_tensor(b_stage[:], b_stage[:], bias_parts[0:3 * NE, :], ALU.subtract))
            for j in (1, 2):
                own.do(pool.tensor_copy(bias_parts[NE * j:NE * j + NE, :], b_stage[NE * j:NE * j + NE, :]))
            two = slice(2 * NE, 3 * NE)
            own.do(pool.tensor_tensor(b_stage[two, :], b_stage[two, :], bias_parts[two, :], ALU.subtract))
            pool.tensor_copy(bias_parts[two, :], b_stage[two, :]).then_inc(parts_made, 1)
            pool.wait_ge(skew_written, 16)
            pool.wait_ge(parts_made, 1)
            own.do(pool.memset(scan_keep[:], 1.0))
            pool.memset(scan_keep[:, 0:1], 0.0).then_inc(scan_set, 1)
            pool.memset(scan_keep[:, META:SMALL], 0.0).then_inc(scan_set, 1)
            pool.memset(scan_keep[:, SMALL:T:CHUNK], 0.0).then_inc(scan_set, 1)

            pool.drain().then_inc(mixer_left, 1)
            pool.wait_ge(mixer_left, 4)
            pool.wait_ge(h2_stored, 16 * NTILE)
            own.do(pool.memset(x_rows[:], 0.0))
            own.do(pool.memset(y_rows[:], 0.0))
            pool.iota(slot_idx[:], pattern=[[0, 4]], base=0, channel_multiplier=1).then_inc(table_made, 1)
            last_token = pool.to_reg(TOK - 1)
            last_slot = pool.to_reg(TOK * TOPK - 1)

            def gather(b):
                pool.wait_ge(idx_ready, b + 1)
                if not (isinstance(b, int) and b == 0):
                    pool.wait_ge(xT_psum, 2 * b)
                pool.sem_inc(rows_asked, 1)
                pool.indirect_dma_start(x_rows[:], None, xn_dram[:, :],
                                        bass.IndirectOffsetOnAxis(ap=token_idx[:, 0:1], axis=0),
                                        bounds_check=last_token, oob_is_err=False).then_inc(gathered, 16)

            def scatter(col, rows_ready, made):
                pool.wait_ge(y_ready, rows_ready)
                pool.wait_ge(aged, made)
                pool.sem_inc(rows_asked, 1)
                pool.indirect_dma_start(slot_dram[:, :], bass.IndirectOffsetOnAxis(ap=slot_idx[:, col:col + 1], axis=0),
                                        y_rows[:], None, bounds_check=last_slot,
                                        oob_is_err=False).then_inc(scattered, 16)

            gather(0)
            gather(1)
            nb = block_count(pool)
            with pool.Fori(1, nb) as b:
                scatter(3, b, b + 1)
                gather(b + 1)
            scatter(3, nb, nb + 1)
            scatter(2, nb + 1, nb + 1)

        @block.sync
        def _(sp):
            sp.dma_start(x_sb[0:META, 0, :], meta).then_inc(ld_x[0], 16)
            sp.dma_start(x_sb[META:SMALL, 0, :], x_sample.rearrange("b s d -> (b s) d")).then_inc(ld_x[0], 16)
            for i in range(PT):
                sp.dma_start(x_sb[:, 1 + i, :], x_prompt[0, P * i:P * i + P, :]).then_inc(ld_x[1 + i], 16)
            for k in range(KT):
                row = w_in[0, P * k:P * k + P, :]
                sp.dma_start(w_in_sb[:, k, 0:SQ], row[:, 0:SQ]).then_inc(ld_win[k], 16)
                sp.dma_start(w_in_sb[:, k, SK:DIN], row[:, SK:DIN]).then_inc(ld_win[k], 16)
                for g in range(KVH):
                    sp.dma_start(w_in_sb[:, k, SQ:SK].rearrange("p (j g n) -> p j g n", j=4, g=KVH)[:, :, g, :],
                                 row[:, SQ + 256 * g:SQ + 256 * g + 256].rearrange("p (j n) -> p j n", j=4)).then_inc(ld_win[k], 16)
            sp.dma_start(states[:], state_gla[0].rearrange("b (r h) k v -> (h k) b r v", h=2)).then_inc(ld_sample, 16)
            sp.wait_ge(rowp_psum, 3 * NTILE)
            sp.dma_start(raw[:, 0, :], w_up[0, 0, 0:P, :]).then_inc(landed[0], 16)
            for src, dst in ((cache_k, k_s), (cache_v, v_s)):
                sp.dma_start(dst[0:WIN - 1, :, :], src[0, :, 1:WIN].rearrange("b j g d -> j b (g d)")).then_inc(ld_sample, 16)
            sp.dma_start(w_out_sb[:], w_out[0].rearrange("(k p) n -> p k n", p=P)).then_inc(ld_wout, 16)
            sp.dma_start(g_ffn_bc[:], g_ffn[0:1, :].to_broadcast([P, D])).then_inc(ld_attn, 16)
            sp.dma_start(w_router_sb[:], w_router[0].rearrange("(k p) n -> p k n", p=P)).then_inc(ld_attn, 16)
            sp.wait_ge(skew_written, 16)
            skewed = bass.AP(tensor=skew_dram.tensor, offset=P - 1, ap=[[QH * 3 * P - 1, P], [3 * P, QH], [1, 2 * P]])
            sp.dma_start(bias_sb[:], skewed).then_inc(skew_read, 16)
            sp.wait_ge(rowsT_copied, 1)
            sp.dma_start(k_s[WIN - 1:WIN, :, :], sk_rows_s[META:SMALL, :]).then_inc(ld_new_rows, 16)
            sp.wait_ge(sv_copied, NTILE)
            sp.dma_start(v_s[WIN - 1:WIN, :, :], sv[META:SMALL, 0, :]).then_inc(ld_new_rows, 16)
            sp.wait_ge(ld_sample, 48)
            sp.wait_ge(ld_new_rows, 32)
            sp.dma_start(ck_s[0].rearrange("b j g d -> j b (g d)"), k_s[:]).then_inc(outputs, 16)
            sp.dma_start(cv_s[0].rearrange("b j g d -> j b (g d)"), v_s[:]).then_inc(outputs, 16)
            sp.dma_start(ck_p[0, 0].rearrange("j g d -> j (g d)"), ck_rows[:]).then_inc(outputs, 16)
            sp.dma_start(cv_p[0, 0].rearrange("j g d -> j (g d)"), sv[:, NTILE - 1, :]).then_inc(outputs, 16)
            sp.dma_start(xr[0:META, :], meta).then_inc(ld_xr, 16)
            sp.dma_start(xr[META:SMALL, :], x_sample.rearrange("b s d -> (b s) d")).then_inc(ld_xr, 16)
            sp.wait_ge(s_state_made, NS)
            sp.dma_start(st_s[0].rearrange("b (r h) k v -> (h k) b r v", h=2), states[:]).then_inc(outputs, 16)
            sp.wait_ge(state_made, 9)
            sp.dma_start(st_p[0, 0].rearrange("(r h) k v -> (h k) r v", h=2), gla_state[:, 8]).then_inc(outputs, 16)
            sp.wait_ge(s_o_copied, 1)
            for g in range(KVH):
                for hh in range(4):
                    h = 4 * g + hh
                    sp.dma_start(mix[META:SMALL, D // 2 + HD * h:D // 2 + HD * h + HD],
                                 o_s[h:h + 1, :, HD * g:HD * g + HD]).then_inc(o_moved, 16)
            for t in range(NTILE):
                n, lo = (NS, META) if t == 0 else (P, 0)
                first = SEQ if t == 0 else P * (t - 1)
                sp.wait_ge(x2_ready, t + 1)
                sp.dma_start(x2_dram[first:first + n, :], xr[lo:lo + n, :]).then_inc(x2_stored, 16)
                sp.wait_ge(h2_ready, t + 1)
                sp.dma_start(xn_dram[first:first + n, :], h2[lo:lo + n, :]).then_inc(h2_stored, 16)
                if t < PT:
                    sp.wait_ge(x2_stored, 16 * (t + 1))
                    sp.dma_start(xr[:], x_prompt[0, P * t:P * t + P, :]).then_inc(ld_xr, 16)
            sp.wait_ge(x2_stored, 16 * NTILE)
            sp.wait_ge(h2_stored, 16 * NTILE)
            sp.wait_ge(outputs, 6 * 16)
            sp.wait_ge(mixer_left, 4)

            def load_up(e, j):
                src = w_up[0, bass.ds(e, 1), P * j:P * j + P, :] if not isinstance(e, int) else w_up[0, e:e + 1, P * j:P * j + P, :]
                sp.dma_start(raw[:, j, :], src.rearrange("a p n -> p (a n)")).then_inc(landed[j], 16)

            def load_down(e, j):
                src = w_down[0, e:e + 1, 2 * P * j:2 * P * (j + 1), :] if isinstance(e, int) else w_down[0, bass.ds(e, 1), 2 * P * j:2 * P * (j + 1), :]
                sp.dma_start(raw[:, UPU + j, :], src.rearrange("a (p r) n -> p (a r n)", r=2)).then_inc(landed[UPU + j], 16)

            for j in range(1, UPU):
                load_up(0, j)
            sp.wait_ge(table_made, 2)
            nb = block_count(sp)
            for j in range(UPU):
                sp.wait_ge(lo_ready, DNU + j + 1)
                load_up(1, j)
            for j in range(DNU):
                load_down(0, j)
            with sp.Fori(2, nb) as b:
                e_up, e_dn = expert(sp, b), expert(sp, b - 1)
                for j in range(UPU):
                    sp.wait_ge(lo_ready, UPB * b - UPB + j + 1)
                    load_up(e_up, j)
                for j in range(DNU):
                    sp.wait_ge(lo_ready, UPB * b - DNU + j + 1)
                    load_down(e_dn, j)
            e_dn = expert(sp, nb - 1)
            for j in range(DNU):
                sp.wait_ge(lo_ready, UPB * nb - DNU + j + 1)
                load_down(e_dn, j)
            sp.wait_ge(lo_ready, UPB * nb + DNU)
            sp.dma_start(g_final_bc[:], g_final.rearrange("(a n) -> a n", a=1).to_broadcast([P, D])).then_inc(ld_gfinal, 16)
            sp.wait_ge(scattered, 16 * nb + 16)
            sp.wait_ge(t_zero, 2)
            for t in range(NTILE):
                n, lo = (NS, META) if t == 0 else (P, 0)
                first = SEQ if t == 0 else P * (t - 1)
                if t >= 3:
                    sp.wait_ge(t_stored[t % 3], 16)
                sp.dma_start(t_slots[t % 3][lo:lo + n, :, :],
                             slot_dram[TOPK * first:TOPK * (first + n), :].rearrange("(p k) n -> p k n", k=TOPK)).then_inc(t_loaded[t % 3], 16)
                sp.dma_start(t_x2[t % 3][lo:lo + n, :], x2_dram[first:first + n, :]).then_inc(t_loaded[t % 3], 16)

        @block.scalar
        def _(act):
            own = Own(act, act_own)
            with nc.allow_non_contiguous_dma(reason="columns of small tables"):
                act.dma_start(tab_sb[:], bias_tab).then_inc(ld_tables, 16)
                act.dma_start(hot_sb[:], bucket_hot).then_inc(ld_tables, 16)
                for j in range(3):
                    act.dma_start(b_stage[NE * j:NE * j + NE, 0:2 * FF], b_up[0]).then_inc(ld_biases, 16)
                    act.dma_start(b_stage[NE * j:NE * j + NE, 2 * FF:3 * FF], b_down[0]).then_inc(ld_biases, 16)
                act.dma_start(g_mixT[:], g_mix[0].rearrange("(k p) -> p k", p=P)).then_inc(ld_small, 16)
                act.dma_start(w_a_sb[:], w_a_up[0]).then_inc(ld_small, 16)
                act.dma_start(b_aT[:], b_a[0].rearrange("(k p) -> p k", p=P)).then_inc(ld_small, 16)
                act.dma_start(g_outT[:, 4:8], g_swa[0].rearrange("(k p) -> p k", p=P)).then_inc(ld_small, 16)
                for h in range(GH):
                    act.dma_start(g_outT[:, h:h + 1], g_gla[0].rearrange("(p a) -> p a", a=1)).then_inc(ld_small, 16)
                act.dma_start(b_rT[:], b_router[0].rearrange("(p a) -> p a", a=1)).then_inc(ld_small, 16)
                act.dma_start(sink_col[:], sinks[0].rearrange("(p a) -> p a", a=1)).then_inc(ld_small, 16)
                act.dma_start(sink_bc[:], sinks[0:1, :].to_broadcast([P, QH])).then_inc(ld_small, 16)
            for t in range(NTILE):
                r = rows[t]
                act.wait_ge(x_var, t + 1)
                act.activation(stat[0:r, 5 + t:6 + t], stat[0:r, t:t + 1], ACT.Sqrt).then_inc(x_root, 1)
                act.wait_ge(x_rstd, t + 1)
                act.activation(x_sb[0:r, t, :], x_sb[0:r, t, :], ACT.Copy, scale=stat[0:r, 10 + t:11 + t]).then_inc(hn_ready, 1)
            act.wait_ge(skew_filled, 1)
            act.wait_ge(flanks, 2)
            act.dma_start(skew_dram, skew_src[:, :, :]).then_inc(skew_written, 16)
            act.wait_ge(ld_small, 11 * 16)

            def copy_colp(n):
                name, _, w = COLP[n // 2]
                half = slice(HALF * (n % 2), HALF * (n % 2) + HALF)
                src = ps[0:w, n % 4, 0:HALF]
                act.wait_ge(colp_psum, n + 1)
                if n == 2:
                    act.wait_ge(parts_made, 1)
                if n == 10:
                    act.wait_ge(skew_written, 16)
                dst, func, kw = {
                    "ga": (gaT[:, half], ACT.Copy, {}), "gk": (gkT[:, int(name[-1]) if name[-1] in "01" else 0, half], ACT.Copy, {}),
                    "gq": (gqT[:, int(name[-1]) if name[-1] in "01" else 0, half], ACT.Copy, {"scale": DK ** -0.5}),
                    "z0": (zT[:, 0, half], ACT.Identity, {"bias": b_aT[:, 0:1]}),
                    "z1": (zT[:, 1, half], ACT.Identity, {"bias": b_aT[:, 1:2]}),
                    "sk": (skT[:, half], ACT.Copy, {}),
                    "sq": (sqT[:, int(name[-1]) if name[-1] in "0123" else 0, half], ACT.Copy, {"scale": SQRT_HD}),
                }[name[:2]]
                act.activation(dst, src, func, **kw).then_inc(colp_copied, 1)

            for n in range(NZ):
                copy_colp(n)
            act.wait_ge(colp_copied, NZ)
            own.do(act.activation(z_l[:], zT[:], ACT.Abs))
            own.do(act.activation(z_l[:], z_l[:], ACT.Exp, scale=-1.0))
            act.activation(z_l[:], z_l[:], ACT.Ln, bias=1.0).then_inc(soft_ready, 1)
            for n in range(NZ, NCOLP):
                copy_colp(n)
            act.wait_ge(decay_ready, 1)
            act.activation(e_pos[:], decay[:], ACT.Exp, scale=1.0 / TAU).then_inc(exps_ready, 1)
            act.activation(kd[:], decay[:], ACT.Exp, scale=-1.0 / TAU).then_inc(exps_ready, 1)
            act.activation(ks[:], ks[:], ACT.Exp, scale=1.0 / TAU).then_inc(exps_ready, 1)
            for t in range(NTILE):
                r = rows[t]
                act.wait_ge(rowp_psum, 3 * t + 1)
                act.activation(gv[0:r, t, :], ps[0:r, 4 + t % 2, :], ACT.Copy).then_inc(gv_copied, 1)
                act.wait_ge(rowp_psum, 3 * t + 2)
                act.activation(gate[0:r, t, :], ps[0:r, 6 + t % 2, :], ACT.Sigmoid).then_inc(sig_made, 1)
                act.wait_ge(rowp_psum, 3 * t + 3)
                act.activation(sv[0:r, t, :], ps[0:r, t % 2, 0:P], ACT.Copy).then_inc(sv_copied, 1)

            for hf in range(2):
                act.wait_ge(ksT_psum, hf + 1)
                act.activation(kT_s[:, 4 * hf:4 * hf + 4, :], ps[:, 4 + hf, :].rearrange("p (b j) -> p b j", b=4),
                               ACT.Copy).then_inc(ksT_copied, 1)
            act.wait_ge(s_shifted, 1)
            act.activation(p_s[:], p_s[:], ACT.Exp).then_inc(s_exp, 1)
            act.activation(small_s[:, 2, :], small_s[:, 1, :], ACT.Exp).then_inc(s_exp, 1)

            def roots(t):
                r = rows[t]
                act.wait_ge(m_var, t + 1)
                act.activation(norm[0:r, 8:13], norm[0:r, 0:5], ACT.Sqrt).then_inc(m_root, 1)

            def softmax(t):
                act.wait_ge(max_ready, t)
                w0 = P - META if t == 1 else 0
                for h in range(QH):
                    act.activation(probs[:, h, w0:2 * P], probs[:, h, w0:2 * P], ACT.Exp, bias=soft[:, 1, h:h + 1],
                                   accum_out=soft[:, 2, h:h + 1]).then_inc(exp_done, 1)
                act.activation(soft[:, 3, :], soft[:, 3, :], ACT.Exp).then_inc(exp_done, 1)

            def move_pT(t):
                for q in range(4):
                    g, part = q // 2, q % 2
                    n = META if t == 1 and part == 0 else P
                    act.wait_ge(pT_psum, 4 * (t - 1) + q + 1)
                    act.activation(pT[0:n, q, :, :], ps[0:n, 4 + part, :].rearrange("p (h q) -> p h q", h=4),
                                   ACT.Copy).then_inc(pT_copied, 1)

            def finish(t):
                r = rows[t]
                act.wait_ge(x2_var, t + 1)
                act.activation(norm[0:r, 25:26], norm[0:r, 24:25], ACT.Sqrt).then_inc(x2_root, 1)
                for hf in range(2):
                    act.wait_ge(h2T_psum, 2 * t + hf + 1)
                    act.activation(mixT[:, 4 * hf:4 * hf + 4, 0:r],
                                   ps[:, 4 + hf, :].rearrange("p (k q) -> p k q", k=4)[:, :, 0:r], ACT.Copy).then_inc(h2T_ready, 1)
                act.wait_ge(lgT_psum, t + 1)
                act.activation(lgT[:, 0:r], ps[0:NE, 2, 0:r], ACT.Identity, bias=b_rT[:]).then_inc(lgT_ready, 1)
                act.wait_ge(top_ready, t + 1)
                act.activation(norm[0:r, 32:36], top_v[0:r, 0:TOPK], ACT.Exp, bias=norm[0:r, 40:41],
                               accum_out=norm[0:r, 41:42]).then_inc(gate_exp, 1)

            for t in range(NTILE):
                if t:
                    move_pT(t)
                roots(t)
                if t < PT:
                    softmax(t + 1)
                finish(t)
            act.drain().then_inc(mixer_left, 1)
            act.wait_ge(mixer_left, 4)

            def hi(slot, unit, q, land):
                act.wait_ge(landed[unit], land)
                act.wait_ge(slot_used, q - RING + 1)
                act.activation(w_hi[:, slot, :], raw[:, unit, :], ACT.Copy).then_inc(hi_ready, 1)

            def x_hi(b):
                for hf in range(2):
                    act.wait_ge(xT_psum, 2 * b + hf + 1)
                    act.activation(xT_hi[:, 4 * hf:4 * hf + 4, :], ps[:, 6 + hf, :].rearrange("p (k q) -> p k q", k=4),
                                   ACT.Copy).then_inc(xT_hi_ready, 1)

            def a_hi(b):
                for hf in range(2):
                    act.wait_ge(aT_psum, 2 * b + hf + 1)
                    act.activation(aT_hi[:, 4 * hf:4 * hf + 4, :], ps[:, 6 + hf, :].rearrange("p (k q) -> p k q", k=4),
                                   ACT.Copy).then_inc(aT_hi_ready, 1)

            def sigmoid(b):
                act.wait_ge(g_ready, b + 1)
                act.activation(act_s[:], act_g[:], ACT.Sigmoid, scale=ALPHA).then_inc(sigm_ready, 1)

            def y_out(used):
                act.wait_ge(slot_used, used)
                act.activation(y_rows[:], ps[:, 4:6, :].rearrange("p a n -> p (a n)"), ACT.Copy).then_inc(y_ready, 1)

            act.sem_inc(y_ready, 1)
            act.sem_inc(hi_ready, DNU)
            x_hi(0)
            for j in range(UPU):
                hi(j % RING, j, DNU + j, 16)
            sigmoid(0)
            x_hi(1)
            nb = block_count(act)
            with act.Fori(1, nb) as b:
                q0 = UPB * b
                for j in range(4):
                    hi(j % RING, j, q0 + j, 16 * b + 16)
                with act.If(b > 1):
                    act.wait_ge(aged, b + 1)
                    y_out(UPB * b)
                for j in range(4, 6):
                    hi(j % RING, j, q0 + j, 16 * b + 16)
                a_hi(b - 1)
                for j in range(6, UPU):
                    hi(j % RING, j, q0 + j, 16 * b + 16)
                for j in range(DNU):
                    hi(j % RING, UPU + j, q0 + UPU + j, 16 * b)
                sigmoid(b)
                x_hi(b + 1)
            q0 = UPB * nb
            act.wait_ge(aged, nb + 1)
            y_out(UPB * nb)
            a_hi(nb - 1)
            for j in range(DNU):
                hi(j % RING, UPU + j, q0 + j, 16 * nb)
            act.wait_ge(scattered, 16 * nb)
            y_out(UPB * nb + DNU)
            for t in range(NTILE):
                act.wait_ge(t_var, t + 1)
                act.activation(t_stat[0:rows[t], t, 1:2], t_stat[0:rows[t], t, 0:1], ACT.Sqrt).then_inc(t_root, 1)
                n, lo = (NS, META) if t == 0 else (P, 0)
                dst = y_s.rearrange("b s d -> (b s) d") if t == 0 else y_p[0, P * (t - 1):P * t, :]
                act.wait_ge(t_y, t + 1)
                act.dma_start(dst, t_x2[t % 3][lo:lo + n, :]).then_inc(t_stored[t % 3], 16)
            for i in range(3):
                act.wait_ge(t_stored[i], 16 * len(range(i, NTILE, 3)))

        @block.vector
        def _(dve):
            own = Own(dve, dve_own)
            step, settle, do = own.step, own.settle, own.do
            junk = gate[:, 0:2, :].rearrange("p a n -> p (a n)")
            for t in range(NTILE):
                r = rows[t]
                dve.wait_ge(ld_x[t], 32 if t == 0 else 16)
                do(dve.tensor_tensor_reduce(junk[0:r, :], x_sb[0:r, t, :], x_sb[0:r, t, :], 1.0, 0.0, ALU.mult, ALU.add,
                                            stat[0:r, t:t + 1]))
                do(dve.tensor_scalar(stat[0:r, t:t + 1], stat[0:r, t:t + 1], 1.0 / D, EPS, ALU.mult, ALU.add))
                dve.sem_inc(x_var, 1)
                dve.wait_ge(x_root, t + 1)
                dve.reciprocal(stat[0:r, 10 + t:11 + t], stat[0:r, 5 + t:6 + t]).then_inc(x_rstd, 1)
            dve.wait_ge(skew_psum, 1)
            for i in range(2):
                do(dve.tensor_copy(skew_src[:, 4 * i:4 * i + 4, P:2 * P], ps[:, i, :].rearrange("p (h x) -> p h x", h=4)))
            do(dve.tensor_copy(bias_s[:], ps[0:QH, 2, 0:WIN]))
            dve.sem_inc(skew_filled, 1)
            dve.wait_ge(ld_small, 11 * 16)
            for t in range(NTILE):
                a, z = cols[t]
                for hf in range(2):
                    dve.wait_ge(hT_psum, 2 * t + hf + 1)
                    dve.tensor_tensor(hT[:, 4 * hf:4 * hf + 4, a:z],
                                      ps[:, 4 + (2 * t + hf) % 4, :].rearrange("p (k q) -> p k q", k=4)[:, :, 0:z - a],
                                      bc(g_mixT[:, 4 * hf:4 * hf + 4], 2, [P, 4, z - a]), ALU.mult).then_inc(hT_ready, 1)
            dve.wait_ge(soft_ready, 1)
            do(dve.scalar_tensor_tensor(z_l[:], zT[:], 0.0, z_l[:], ALU.min, ALU.subtract))
            dve.wait_ge(scan_set, 3)
            for r in range(2):
                step(dve.tensor_tensor_scan(decay[:, r, :], scan_keep[:], z_l[:, r, :], 0.0, ALU.mult, ALU.add))
            settle()
            for r in range(2):
                step(dve.tensor_tensor(ks[:, r, 0:META], decay[:, r, META - 1:META].to_broadcast([P, META]),
                                       decay[:, r, 0:META], ALU.subtract))
                d = decay[:, r, SMALL:T].rearrange("p (c s) -> p c s", s=CHUNK)
                step(dve.tensor_tensor(ks[:, r, SMALL:T].rearrange("p (c s) -> p c s", s=CHUNK),
                                       d[:, :, CHUNK - 1:CHUNK].to_broadcast([P, SEQ // CHUNK, CHUNK]), d, ALU.subtract))
            step(dve.memset(ks[:, :, META:SMALL], 0.0))
            settle()
            dve.sem_inc(decay_ready, 1)
            dve.wait_ge(exps_ready, 3)
            step(dve.tensor_tensor(qd[:], gqT[:], e_pos[:], ALU.mult))
            step(dve.tensor_tensor(kd[:], gkT[:], kd[:], ALU.mult))
            step(dve.tensor_tensor(ks[:], gkT[:], ks[:], ALU.mult))
            settle()
            dve.sem_inc(gla_ready, 1)
            for t in range(NTILE):
                r = rows[t]
                dve.wait_ge(sig_made, t + 1)
                dve.tensor_tensor(gate[0:r, t, :], ps[0:r, 6 + t % 2, :], gate[0:r, t, :], ALU.mult).then_inc(gate_made, 1)
            dve.wait_ge(consts, NCONST)
            dve.wait_ge(rowsT_psum, 1)
            step(dve.tensor_copy(k_rows_s[:], ps[0:SMALL, 0, 0:2 * P].rearrange("p (r x) -> p r x", r=2)))
            step(dve.tensor_copy(sk_rows_s[:], ps[0:SMALL, 0, 2 * P:3 * P]))
            step(dve.tensor_copy(ck_rows[:], ps[:, 0, 3 * P:4 * P]))
            step(dve.tensor_copy(ks_rows[0:META, 0], ps[0:META, 1, 0:2 * P].rearrange("p (r x) -> p r x", r=2)))
            step(dve.tensor_copy(ks_rows[:, 1:5], ps[:, 2:4, :].rearrange("p a (t r x) -> p (a t) r x", t=2, r=2)))
            settle()
            dve.sem_inc(rowsT_copied, 1)
            step(dve.memset(q_diag[:], 0.0))
            step(dve.memset(q_swa[:], 0.0))
            for b in range(NS):
                step(dve.tensor_scalar(k_diag[:, b, :], k_rows_s[:].rearrange("p r x -> p (r x)"),
                                       ident[0:SMALL, META + b:META + b + 1], None, ALU.mult))
            settle()
            for r in range(2):
                flat = q_diag[:, r].rearrange("p b c -> p (b c)")
                step(dve.tensor_copy(flat[:, META:META + (SMALL + 1) * (NS - 1) + 1:SMALL + 1], gqT[:, r, META:SMALL]))
            for g in range(KVH):
                half = slice(HD * g, HD * g + HD)
                step(dve.tensor_copy(q_swa[half, :, 4 * g:4 * g + 4],
                                     sqT[half, :, META:SMALL].rearrange("p j b -> p b j")))
            settle()
            dve.sem_inc(diags_made, 1)
            for c in range(9):
                dve.wait_ge(kv_psum, c + 1)
                src = ps[:, 4 + c % 4, 0:256].rearrange("p (r v) -> p r v", r=2)
                if c == 0:
                    step(dve.tensor_copy(gla_state[:, 0], src))
                else:
                    end = SMALL + CHUNK * c - 1
                    for r in range(2):
                        step(dve.scalar_tensor_tensor(gla_state[:, c, r, :], gla_state[:, c - 1, r, :],
                                                      e_pos[:, r, end:end + 1], src[:, r, :], ALU.mult, ALU.add))
                settle()
                dve.sem_inc(state_made, 1)
            dve.wait_ge(ld_sample, 48)
            for b in range(NS):
                dve.wait_ge(outer_psum, b // 2 + 1)
                for r in range(2):
                    src = ps[:, b // 2, 256 * (b % 2) + P * r:256 * (b % 2) + P * r + P]
                    step(dve.scalar_tensor_tensor(states[:, b, r, :], states[:, b, r, :],
                                                  e_pos[:, r, META + b:META + b + 1], src, ALU.mult, ALU.add))
                settle()
                dve.sem_inc(s_state_made, 1)
            dve.wait_ge(s_score_psum, 1)
            do(dve.tensor_tensor(p_s[:], ps[0:QH, 0:2, :].rearrange("p a (b j) -> p (a b) j", b=4),
                                 bc(bias_s[:], 1, [QH, NS, WIN]), ALU.add))
            do(dve.tensor_reduce(small_s[:, 0, :], p_s[:], AX, ALU.max))
            do(dve.tensor_scalar(small_s[:, 0, :], small_s[:, 0, :], sink_col[:], None, ALU.max))
            step(dve.tensor_scalar(small_s[:, 1, :], small_s[:, 0, :], -1.0, sink_col[:], ALU.mult, ALU.add))
            step(dve.tensor_tensor(p_s[:], p_s[:], bc(small_s[:, 0, :], 2, [QH, NS, WIN]), ALU.subtract))
            settle()
            dve.sem_inc(s_shifted, 1)
            dve.wait_ge(s_exp, 2)
            do(dve.tensor_reduce(small_s[:, 3, :], p_s[:], AX, ALU.add))
            do(dve.tensor_tensor(small_s[:, 3, :], small_s[:, 3, :], small_s[:, 2, :], ALU.add))
            do(dve.reciprocal(small_s[:, 3, :], small_s[:, 3, :]))
            dve.tensor_tensor(p_s[:], p_s[:], bc(small_s[:, 3, :], 2, [QH, NS, WIN]), ALU.mult).then_inc(s_probs, 1)
            dve.wait_ge(s_pT_psum, 1)
            dve.tensor_copy(pT_s[:], ps[:, 2, 0:NS * QH].rearrange("p (b h) -> p b h", b=NS)).then_inc(s_pT_copied, 1)
            dve.wait_ge(s_pv_psum, 1)
            do(dve.memset(mix[0:SMALL, D // 2:D], 0.0))
            dve.tensor_copy(o_s[:], ps[0:QH, 0:2, :].rearrange("p a (b x) -> p (a b) x", b=4)).then_inc(s_o_copied, 1)

            def take_gla(t):
                r = rows[t]
                if t:
                    dve.wait_ge(a_psum, t)
                    for i in range(2):
                        dve.tensor_tensor(a_gla[:, i:GH:2, :], ps[:, 6 + i, 0:256].rearrange("p (h q) -> p h q", h=2),
                                          bc(same_chunk[:], 1, [P, 2, P]), ALU.mult).then_inc(a_masked, 1)
                dve.wait_ge(o_psum, t + 1)
                if t:
                    dve.wait_ge(mixT_psum, 2 * t)
                for i in range(2):
                    dve.tensor_copy(mix[0:r, 0:D // 2].rearrange("p (h v) -> p h v", h=GH)[:, i:GH:2, :],
                                    ps[0:r, 6 + i, 256:512].rearrange("p (h v) -> p h v", h=2)).then_inc(o_copied, 1)

            def scores(t):
                w0 = P - META if t == 1 else 0
                if t == 1:
                    dve.wait_ge(skew_read, 16)
                dve.wait_ge(score_psum, t)
                if t == 1:
                    dve.wait_ge(s_pT_copied, 1)
                for i in range(4):
                    step(dve.tensor_tensor(probs[:, 2 * i:2 * i + 2, w0:2 * P],
                                           ps[:, i, :].rearrange("p (h j) -> p h j", h=2)[:, :, w0:2 * P],
                                           bias_sb[:, 2 * i:2 * i + 2, w0:2 * P], ALU.add))
                settle()
                do(dve.tensor_reduce(soft[:, 0, :], probs[:, :, w0:2 * P], AX, ALU.max))
                do(dve.tensor_tensor(soft[:, 0, :], soft[:, 0, :], sink_bc[:], ALU.max))
                step(dve.tensor_scalar(soft[:, 1, :], soft[:, 0, :], -1.0, None, ALU.mult))
                step(dve.tensor_tensor(soft[:, 3, :], sink_bc[:], soft[:, 0, :], ALU.subtract))
                settle()
                dve.sem_inc(max_ready, 1)

            def make_mix(t):
                r = rows[t]
                scratch = h2[0:r, 0:D // 2]
                if t == 0:
                    dve.wait_ge(o_moved, 16 * QH)
                else:
                    dve.wait_ge(exp_done, (QH + 1) * t)
                    do(dve.tensor_tensor(soft[:, 0, :], soft[:, 2, :], soft[:, 3, :], ALU.add))
                    do(dve.reciprocal(soft[:, 0, :], soft[:, 0, :]))
                    dve.wait_ge(pv_psum, t)
                    for g in range(KVH):
                        step(dve.tensor_tensor(
                            mix[:, D // 2 + 256 * g:D // 2 + 256 * g + 256].rearrange("p (h x) -> p h x", h=4),
                            ps[:, g, :].rearrange("p (h x) -> p h x", h=4)[:, :, HD * g:HD * g + HD],
                            bc(soft[:, 0, 4 * g:4 * g + 4], 2, [P, 4, HD]), ALU.mult))
                    settle()
                    dve.sem_inc(pv_copied, 1)
                    dve.wait_ge(h2_stored, 16 * t)
                dve.wait_ge(o_copied, 2 * t + 2)
                do(dve.tensor_tensor(scratch, mix[0:r, 0:D // 2], mix[0:r, 0:D // 2], ALU.mult))
                do(dve.tensor_reduce(norm[0:r, 0:4], scratch.rearrange("p (h v) -> p h v", h=GH), AX, ALU.add))
                do(dve.tensor_tensor_reduce(scratch, mix[0:r, D // 2:D], mix[0:r, D // 2:D], 1.0, 0.0, ALU.mult, ALU.add,
                                            norm[0:r, 4:5]))
                step(dve.tensor_scalar(norm[0:r, 0:4], norm[0:r, 0:4], 1.0 / DV, EPS, ALU.mult, ALU.add))
                step(dve.tensor_scalar(norm[0:r, 4:5], norm[0:r, 4:5], 1.0 / (QH * HD), EPS, ALU.mult, ALU.add))
                settle()
                dve.sem_inc(m_var, 1)
                dve.wait_ge(m_root, t + 1)
                do(dve.reciprocal(norm[0:r, 16:21], norm[0:r, 8:13]))
                for h in range(GH):
                    m = mix[0:r, DV * h:DV * h + DV]
                    step(dve.scalar_tensor_tensor(m, m, norm[0:r, 16 + h:17 + h], gate[0:r, t, DV * h:DV * h + DV],
                                                  ALU.mult, ALU.mult))
                m = mix[0:r, D // 2:D]
                step(dve.tensor_scalar(m, m, norm[0:r, 20:21], None, ALU.mult))
                settle()
                dve.sem_inc(mix_ready, 1)

            def take_mixT(t):
                r = rows[t]
                for hf in range(2):
                    dve.wait_ge(mixT_psum, 2 * t + hf + 1)
                    if t:
                        dve.wait_ge(lgT_psum, t)
                    dve.tensor_tensor(mixT[:, 4 * hf:4 * hf + 4, 0:r],
                                      ps[:, 4 + hf, :].rearrange("p (k q) -> p k q", k=4)[:, :, 0:r],
                                      bc(g_outT[:, 4 * hf:4 * hf + 4], 2, [P, 4, r]), ALU.mult).then_inc(mixT_ready, 1)

            def residual(t):
                r = rows[t]
                dve.wait_ge(ld_xr, 16 * (t + 2))
                dve.wait_ge(out_psum, t + 1)
                do(dve.tensor_tensor(xr[0:r, :], ps[0:r, 6:8, :].rearrange("p a n -> p (a n)"), xr[0:r, :], ALU.add))
                dve.sem_inc(x2_ready, 1)
                do(dve.tensor_tensor_reduce(h2[0:r, :], xr[0:r, :], xr[0:r, :], 1.0, 0.0, ALU.mult, ALU.add, norm[0:r, 24:25]))
                do(dve.tensor_scalar(norm[0:r, 24:25], norm[0:r, 24:25], 1.0 / D, EPS, ALU.mult, ALU.add))
                dve.sem_inc(x2_var, 1)
                dve.wait_ge(x2_root, t + 1)
                do(dve.reciprocal(norm[0:r, 26:27], norm[0:r, 25:26]))
                if t == 0:
                    dve.wait_ge(ld_attn, 32)
                dve.scalar_tensor_tensor(h2[0:r, :], xr[0:r, :], norm[0:r, 26:27], g_ffn_bc[0:r, :], ALU.mult,
                                         ALU.mult).then_inc(h2_ready, 1)

            def route(t):
                r = rows[t]
                dve.wait_ge(lg_psum, t + 1)
                lg = ps[0:r, 3, 0:NE]
                do(dve.max(top_v[0:r, :], lg))
                step(dve.max_index(top_i[0:r, :], top_v[0:r, :], lg))
                step(dve.tensor_scalar(norm[0:r, 40:41], top_v[0:r, 0:1], -1.0, None, ALU.mult))
                settle()
                dve.sem_inc(top_ready, 1)
                do(dve.tensor_copy(top_f[0:r, :], top_i[0:r, :]))
                do(dve.tensor_tensor(one_hot[0:r], bc(slots_row[0:r, 0:NE], 1, [r, TOPK, NE]),
                                     bc(top_f[0:r, 0:TOPK], 2, [r, TOPK, NE]), ALU.is_equal))
                if t == 0:
                    do(dve.tensor_scalar(one_hot[0:r], one_hot[0:r], row_ok[:], None, ALU.mult))
                step(dve.tensor_tensor(one_hot_k[0:r], one_hot[0:r], bc(slots_row[0:r, 0:TOPK], 2, [r, TOPK, NE]), ALU.mult))
                with nc.allow_low_precision(reason="zeros and ones"):
                    step(dve.tensor_reduce(m_keep[0:r, t, :], one_hot[0:r].rearrange("p k e -> p e k"), AX, ALU.add))
                settle()
                with nc.allow_low_precision(reason="integers up to three"):
                    step(dve.tensor_reduce(slot_table[0:r, t, :, 2], one_hot_k[0:r].rearrange("p k e -> p e k"), AX, ALU.add))
                dve.wait_ge(gate_exp, t + 1)
                do(dve.reciprocal(norm[0:r, 42:43], norm[0:r, 41:42]))
                step(dve.tensor_scalar(gates[0:r, t, :], norm[0:r, 32:36], norm[0:r, 42:43], None, ALU.mult))
                settle()
                dve.sem_inc(routed, 1)

            take_gla(0)
            for t in range(NTILE):
                make_mix(t)
                take_mixT(t)
                if t < PT:
                    scores(t + 1)
                residual(t)
                if t < PT:
                    take_gla(t + 1)
                route(t)

            dve.wait_ge(pos_psum, 1)
            do(dve.scalar_tensor_tensor(pos_table[:], ps[:, 0, 0:NTILE * NE].rearrange("p (t e) -> p t e", t=NTILE), 1.0,
                                        m_keep[:], ALU.add, ALU.mult))
            do(dve.tensor_scalar(pos_table[:], pos_table[:], -1.0, None, ALU.add))
            count = ps[:, 0, NTILE * NE:(NTILE + 1) * NE]
            for m in range(4):
                step(dve.tensor_scalar(over[:, m, :], count, float(P * (m + 1)), None, ALU.is_gt))
            settle()
            flat, flat_end = over[:].rearrange("p m e -> p (m e)"), over_end[:].rearrange("p m e -> p (m e)")
            ones_row = one_hot_k[:].rearrange("p k e -> p (k e)")
            do(dve.memset(ones_row, 1.0))
            do(dve.tensor_tensor_scan(flat_end, ones_row, flat, 0.0, ALU.mult, ALU.add))
            step(dve.tensor_scalar(norm[:, 0:1], flat_end[:, 4 * NE - 1:4 * NE], float(NE - 2), None, ALU.add))
            settle()
            do(dve.tensor_tensor(flat_end, flat_end, flat, ALU.subtract))
            do(dve.scalar_tensor_tensor(flat, flat_end, pidx[:], flat, ALU.is_equal, ALU.mult))
            do(dve.tensor_tensor(over_end[:], over[:], bc(slots_row[:, 0:NE], 1, [P, 4, NE]), ALU.mult))
            step(dve.tensor_reduce(norm[:, 1:2], flat_end, AX, ALU.add))
            step(dve.tensor_reduce(norm[:, 4:8], over[:], AX, ALU.add))
            settle()
            do(dve.tensor_tensor(norm[:, 4:8], norm[:, 4:8], slots_row[:, 1:5], ALU.mult))
            do(dve.tensor_reduce(norm[:, 2:3], norm[:, 4:8], AX, ALU.add))
            do(dve.tensor_scalar(norm[:, 2:3], norm[:, 2:3], float(P), None, ALU.mult))
            for i in range(2):
                step(dve.tensor_scalar(one_hot[0:16, i, 0:16], ident[0:16, 0:16], norm[0:16, 1 + i:2 + i], None, ALU.mult))
            settle()
            dve.sem_inc(over_made, 1)
            step(dve.memset(blk_expert[:], 0.0))
            step(dve.memset(blk_start[:], 0.0))
            settle()
            step(dve.tensor_copy(blk_expert[:, 0:NE], slots_row[:, 0:NE]))
            dve.wait_ge(over_psum, 1)
            step(dve.tensor_copy(blk_expert[:, NE:NE + 16], ps[:, 1, 0:16]))
            step(dve.tensor_copy(blk_start[:, NE:NE + 16], ps[:, 1, 16:32]))
            settle()
            step(dve.tensor_copy(blk_row[0:1, 0:BLKS], blk_expert[0:1, :]))
            step(dve.tensor_copy(blk_row[0:1, BLKS:BLKS + 1], norm[0:1, 0:1]))
            settle()
            dve.sem_inc(table_made, 1)
            dve.sem_inc(mixer_left, 1)
            dve.wait_ge(mixer_left, 4)
            dve.wait_ge(table_made, 2)
            OWN0 = own.n

            def find_slots(o, b):
                e = expert(dve, b)
                col = slice(e, e + 1) if isinstance(e, int) else bass.ds(e, 1)
                bcol = slice(b, b + 1) if isinstance(b, int) else bass.ds(b, 1)
                o.step(dve.tensor_scalar(shifted[:].unsqueeze(2), pos_table[:, :, col], blk_start[:, bcol], None, ALU.subtract))
                o.step(dve.tensor_copy(slot_cols[:].unsqueeze(2), slot_table[:, :, col, :]))
                o.settle()
                dve.tensor_tensor(hit[:], bc(slots_row[:], 1, [P, NTILE, P]), bc(shifted[:], 2, [P, NTILE, P]),
                                  ALU.is_equal).then_inc(hit_ready, 1)

            def indices(o, b):
                dve.wait_ge(list_psum, b + 1)
                o.do(dve.tensor_copy(found[:], ps[:, 6, 0:4]))
                o.step(dve.tensor_scalar(empty[:], found[:, 3:4], -FAR, FAR, ALU.mult, ALU.add))
                o.step(dve.scalar_tensor_tensor(token_f[:], found[:, 1:2], 16.0, found[:, 0:1], ALU.mult, ALU.add))
                o.settle()
                o.step(dve.scalar_tensor_tensor(slot_f[:], token_f[:], float(TOPK), found[:, 2:3], ALU.mult, ALU.add))
                o.step(dve.tensor_tensor(token_idx[:], token_f[:], empty[:], ALU.add))
                o.settle()
                dve.tensor_tensor(slot_idx[:, 0:1], slot_f[:], empty[:], ALU.add).then_inc(idx_ready, 1)

            def age_indices(o, made):
                dve.wait_ge(idx_ready, made)
                o.do(dve.tensor_copy(slot_tmp[:], slot_idx[:, 0:3]))
                dve.tensor_copy(slot_idx[:, 1:4], slot_tmp[:]).then_inc(aged, 1)
                dve.wait_ge(aged, made)

            def select(dst, b, s):
                bcol = slice(b, b + 1) if isinstance(b, int) else bass.ds(b, 1)
                dve.tensor_tensor(dst[:], expert_of_row[:].to_broadcast([P, P]), blk_expert[:, bcol].to_broadcast([P, P]),
                                  ALU.is_equal).then_inc(s, 1)

            def lo(slot, unit, q):
                dve.wait_ge(hi_ready, q + 1)
                ins = dve.tensor_tensor(w_lo[:, slot, :], raw[:, unit, :], w_hi[:, slot, :].bitcast(F32), ALU.subtract)
                ins.then_inc(lo_ready, 1)

            def x_lo(b):
                for hf in range(2):
                    dve.wait_ge(xT_hi_ready, 2 * b + hf + 1)
                    dve.tensor_tensor(xT_lo[:, 4 * hf:4 * hf + 4, :], ps[:, 6 + hf, :].rearrange("p (k q) -> p k q", k=4),
                                      xT_hi[:, 4 * hf:4 * hf + 4, :].bitcast(F32), ALU.subtract).then_inc(xT_ready, 1)

            def a_lo(b):
                for hf in range(2):
                    dve.wait_ge(aT_hi_ready, 2 * b + hf + 1)
                    dve.tensor_tensor(aT_lo[:, 4 * hf:4 * hf + 4, :], ps[:, 6 + hf, :].rearrange("p (k q) -> p k q", k=4),
                                      aT_hi[:, 4 * hf:4 * hf + 4, :].bitcast(F32), ALU.subtract).then_inc(aT_ready, 1)

            def swiglu(o, b):
                dve.wait_ge(slot_used, up_end(b))
                dve.tensor_scalar(act_g[:], ps[:, 0:2, :].rearrange("p a n -> p (a n)"), LIMIT, None, ALU.min).then_inc(g_ready, 1)
                dve.tensor_scalar(act_l[:], ps[:, 2:4, :].rearrange("p a n -> p (a n)"), LIMIT, -LIMIT, ALU.min,
                                  ALU.max).then_inc(up_read, 1)
                dve.wait_ge(sigm_ready, b + 1)
                o.do(dve.tensor_tensor(act_s[:], act_g[:], act_s[:], ALU.mult))
                dve.wait_ge(up_read, b + 1)
                dve.scalar_tensor_tensor(act_g[:], act_l[:], 1.0, act_s[:], ALU.add, ALU.mult).then_inc(a_ready, 1)

            dve.sem_inc(lo_ready, DNU)
            find_slots(own, 0)
            indices(own, 0)
            age_indices(own, 1)
            select(sel_up, 0, sel_up_ready)
            x_lo(0)
            find_slots(own, 1)
            for j in range(4):
                lo(j % RING, j, DNU + j)
            indices(own, 1)
            for j in range(4, UPU):
                lo(j % RING, j, DNU + j)
            dve.wait_ge(up_bias_done, 1)
            select(sel_up, 1, sel_up_ready)
            select(sel_dn, 0, sel_dn_ready)
            swiglu(own, 0)
            x_lo(1)
            age_indices(own, 2)
            before_loop = own.n
            nb = block_count(dve)
            with dve.Fori(1, nb) as b:
                STEPS = 9
                o = Own(dve, dve_own, b * STEPS + (before_loop - STEPS))
                q0 = UPB * b
                find_slots(o, b + 1)
                for j in range(5):
                    lo(j % RING, j, q0 + j)
                indices(o, b + 1)
                lo(5 % RING, 5, q0 + 5)
                dve.wait_ge(up_bias_done, b + 1)
                select(sel_up, b + 1, sel_up_ready)
                lo(6 % RING, 6, q0 + 6)
                a_lo(b - 1)
                lo(7 % RING, 7, q0 + 7)
                for j in range(DNU):
                    lo(j % RING, UPU + j, q0 + UPU + j)
                swiglu(o, b)
                x_lo(b + 1)
                dve.wait_ge(dn_bias_done, b)
                select(sel_dn, b, sel_dn_ready)
                dve.wait_ge(scattered, 16 * b)
                age_indices(o, b + 2)
                assert o.n == STEPS, o.n
            q0 = UPB * nb
            a_lo(nb - 1)
            for j in range(DNU):
                lo(j % RING, UPU + j, q0 + j)
            own = Own(dve, dve_own, nb * STEPS + (before_loop - STEPS))
            step, do, settle = own.step, own.do, own.settle
            dve.wait_ge(slot_used, UPB * nb + DNU)
            step(dve.memset(t_slots[0][0:META, :, :], 0.0))
            step(dve.memset(t_x2[0][0:META, :], 0.0))
            settle()
            dve.sem_inc(t_zero, 2)
            for t in range(NTILE):
                r = rows[t]
                x2, y4 = t_x2[t % 3], t_slots[t % 3]
                dve.wait_ge(t_loaded[t % 3], 32 * (t // 3 + 1))
                for k in range(TOPK):
                    do(dve.scalar_tensor_tensor(x2[0:r, :], y4[0:r, k, :], gates[0:r, t, k:k + 1], x2[0:r, :], ALU.mult, ALU.add))
                do(dve.tensor_tensor_reduce(t_sq[0:r, :], x2[0:r, :], x2[0:r, :], 1.0, 0.0, ALU.mult, ALU.add, t_stat[0:r, t, 0:1]))
                do(dve.tensor_scalar(t_stat[0:r, t, 0:1], t_stat[0:r, t, 0:1], 1.0 / D, EPS, ALU.mult, ALU.add))
                dve.sem_inc(t_var, 1)
                dve.wait_ge(t_root, t + 1)
                do(dve.reciprocal(t_stat[0:r, t, 2:3], t_stat[0:r, t, 1:2]))
                dve.wait_ge(ld_gfinal, 16)
                dve.scalar_tensor_tensor(x2[0:r, :], x2[0:r, :], t_stat[0:r, t, 2:3], g_final_bc[0:r, :], ALU.mult,
                                         ALU.mult).then_inc(t_y, 1)

        @block.tensor
        def _(pe):
            mm = nc.tensor.matmul
            pe.wait_ge(ld_tables, 32)
            for h in range(QH):
                mm(ps[:, h // 4, P * (h % 4):P * (h % 4) + P], tab_sb[:, h:h + 1].to_broadcast([BUCKETS, P]), hot_sb[:],
                   start=True, stop=True)
            mm(ps[0:QH, 2, 0:WIN], tab_sb[:], hot_sb[:], start=True, stop=True).then_inc(skew_psum, 1)
            pe.wait_ge(consts, 1)
            for t in range(NTILE):
                r = rows[t]
                pe.wait_ge(hn_ready, t + 1)
                for hf in range(2):
                    n = 2 * t + hf
                    if n >= 4:
                        pe.wait_ge(hT_ready, n - 3)
                    for k in range(4):
                        ins = pe.transpose(ps[:, 4 + n % 4, P * k:P * k + r], x_sb[0:r, t, P * (4 * hf + k):P * (4 * hf + k + 1)],
                                           ident[0:r, 0:r])
                    ins.then_inc(hT_psum, 1)
            pe.wait_ge(hT_ready, 2 * NTILE)
            pe.wait_ge(skew_filled, 1)
            for n in range(NCOLP):
                name, c0, w = COLP[n // 2]
                half = slice(HALF * (n % 2), HALF * (n % 2) + HALF)
                dst = ps[0:w, n % 4, 0:HALF]
                if n >= 4:
                    pe.wait_ge(colp_copied, n - 3)
                if name[0] == "z":
                    if n == 10:
                        pe.wait_ge(ld_small, 11 * 16)
                    mm(dst, w_a_sb[:, c0:c0 + P], gaT[:, half], start=True, stop=True).then_inc(colp_psum, 1)
                    continue
                for k in range(KT):
                    if n == 0:
                        pe.wait_ge(ld_win[k], 64)
                    ins = mm(dst, w_in_sb[:, k, c0:c0 + w], hT[:, k, half], start=(k == 0), stop=(k == KT - 1))
                ins.then_inc(colp_psum, 1)
            for t in range(NTILE):
                a, z = cols[t]
                r = z - a
                for bank, c0, w, freed in ((4 + t % 2, GV, GH * DV, gv_copied), (6 + t % 2, GR, GH * DV, gate_made),
                                           (t % 2, SV, P, sv_copied)):
                    if t >= 2:
                        pe.wait_ge(freed, t - 1)
                    elif w == P:
                        pe.wait_ge(colp_copied, NCOLP)
                    for k in range(KT):
                        ins = mm(ps[0:r, bank, 0:w], hT[:, k, a:z], w_in_sb[:, k, c0:c0 + w], start=(k == 0), stop=(k == KT - 1))
                    ins.then_inc(rowp_psum, 1)
            pe.wait_ge(gla_ready, 1)
            pe.wait_ge(sv_copied, NTILE)
            pe.wait_ge(gv_copied, NTILE)
            pe.wait_ge(gate_made, NTILE)
            for r in range(2):
                pe.transpose(ps[0:SMALL, 0, P * r:P * r + P], gkT[:, r, 0:SMALL], ident[:])
            pe.transpose(ps[0:SMALL, 0, 2 * P:3 * P], skT[:, 0:SMALL], ident[:])
            pe.transpose(ps[:, 0, 3 * P:4 * P], skT[:, T - WIN:T], ident[:])
            for r in range(2):
                pe.transpose(ps[0:META, 1, P * r:P * r + P], ks[:, r, 0:META], ident[:])
            for i in range(PT):
                for r in range(2):
                    ins = pe.transpose(ps[:, 2 + i // 2, 256 * (i % 2) + P * r:256 * (i % 2) + P * r + P],
                                       ks[:, r, SMALL + P * i:SMALL + P * i + P], ident[:])
            ins.then_inc(rowsT_psum, 1)
            pe.wait_ge(rowsT_copied, 1)
            for c in range(9):
                if c >= 4:
                    pe.wait_ge(state_made, c - 3)
                t, r0, n = (0, 0, META) if c == 0 else ((c + 1) // 2, CHUNK * ((c - 1) % 2), CHUNK)
                for h in range(GH):
                    part, pair = head(h)
                    ins = mm(ps[part, 4 + c % 4, DV * pair:DV * pair + DV], ks_rows[r0:r0 + n, t, pair, part],
                             gv[r0:r0 + n, t, DV * h:DV * h + DV], start=True, stop=True)
                ins.then_inc(kv_psum, 1)
            pe.wait_ge(diags_made, 1)
            for b in range(NS):
                for h in range(GH):
                    part, pair = head(h)
                    at = 256 * (b % 2) + DV * pair
                    ins = mm(ps[part, b // 2, at:at + DV], k_diag[:, b, DK * h:DK * h + DK], gv[0:SMALL, 0, DV * h:DV * h + DV],
                             start=True, stop=True)
                if b % 2:
                    ins.then_inc(outer_psum, 1)
            pe.wait_ge(ld_sample, 48)
            pe.wait_ge(ld_new_rows, 32)
            pe.wait_ge(state_made, 9)
            for hf in range(2):
                for i in range(4):
                    ins = pe.transpose(ps[:, 4 + hf, P * i:P * i + P], k_s[:, 4 * hf + i, :], ident[:])
                ins.then_inc(ksT_psum, 1)
            pe.wait_ge(s_state_made, NS)
            pe.wait_ge(ksT_copied, 2)
            for b in range(NS):
                ins = mm(ps[0:QH, b // 4, P * (b % 4):P * (b % 4) + P], q_swa[:, b, :], kT_s[:, b, :], start=True, stop=True)
            ins.then_inc(s_score_psum, 1)
            pe.wait_ge(state_made, 9)
            for h in range(GH):
                part, pair = head(h)
                for b in range(NS):
                    ins = mm(ps[0:SMALL, 6 + h % 2, 256 + DV * pair:256 + DV * pair + DV], q_diag[part, pair, b, :], states[part, b, pair, :],
                             start=(b == 0), stop=(b == NS - 1))
            ins.then_inc(o_psum, 1)
            pe.wait_ge(s_probs, 1)
            for b in range(NS):
                ins = pe.transpose(ps[:, 2, QH * b:QH * b + QH], p_s[:, b, :], ident[0:QH, 0:QH])
            ins.then_inc(s_pT_psum, 1)
            pe.wait_ge(s_pT_copied, 1)
            for b in range(NS):
                ins = mm(ps[0:QH, b // 4, P * (b % 4):P * (b % 4) + P], pT_s[:, b, :], v_s[:, b, :], start=True, stop=True)
            ins.then_inc(s_pv_psum, 1)

            def score(t):
                if t == 1:
                    pe.wait_ge(s_o_copied, 1)
                else:
                    pe.wait_ge(pv_copied, t - 1)
                    pe.wait_ge(routed, t - 1)
                a, z = cols[t]
                for h in range(QH):
                    g = h // 4
                    half = slice(HD * g, HD * g + HD)
                    q = sqT[half, h % 4, a:z]
                    dst = ps[:, h // 2, 256 * (h % 2):256 * (h % 2) + 256]
                    if t == 1:
                        mm(dst[:, P - META:P], q, skT[half, 0:META], start=True, stop=True)
                        ins = mm(dst[:, P:2 * P], q, skT[half, a:z], start=True, stop=True)
                    else:
                        ins = mm(dst, q, skT[half, a - P:z], start=True, stop=True)
                ins.then_inc(score_psum, 1)

            def gla(t):
                pe.wait_ge(x2_ready, t)
                a, z = cols[t]
                for h in range(GH):
                    part, pair = head(h)
                    ins = mm(ps[:, 6 + h % 2, P * pair:P * pair + P], kd[part, pair, a:z], qd[part, pair, a:z], start=True, stop=True)
                ins.then_inc(a_psum, 1)
                pe.wait_ge(a_masked, 2 * t)
                for h in range(GH):
                    part, pair = head(h)
                    o_at = slice(256 + DV * pair, 256 + DV * pair + DV)
                    mm(ps[:, 6 + h % 2, o_at], a_gla[:, h, :], gv[:, t, DV * h:DV * h + DV], start=True, stop=False,
                       skip_group_check=True)
                    for c in range(2):
                        ins = mm(ps[CHUNK * c:CHUNK * c + CHUNK, 6 + h % 2, o_at],
                                 qd[part, pair, a + CHUNK * c:a + CHUNK * c + CHUNK], gla_state[part, 2 * (t - 1) + c, pair, :],
                                 start=False, stop=True, skip_group_check=True)
                ins.then_inc(o_psum, 1)

            def attend(t):
                def turn(g):
                    for part in range(2):
                        q = 4 * (t - 1) + 2 * g + part
                        c0, n = (P - META, META) if t == 1 and part == 0 else (P * part, P)
                        if g:
                            pe.wait_ge(pT_copied, q - 1)
                        for i in range(4):
                            ins = pe.transpose(ps[0:n, 4 + part, P * i:P * i + P], probs[:, 4 * g + i, c0:c0 + n], ident[:])
                        ins.then_inc(pT_psum, 1)

                def weigh(g):
                    pe.wait_ge(pT_copied, 4 * (t - 1) + 2 * g + 2)
                    n = META if t == 1 else P
                    for i in range(4):
                        dst = ps[:, g, P * i:P * i + P]
                        mm(dst, pT[0:n, 2 * g, i, :], sv[0:n, t - 1, :], start=True, stop=False)
                        ins = mm(dst, pT[:, 2 * g + 1, i, :], sv[:, t, :], start=False, stop=True)
                    return ins

                pe.wait_ge(exp_done, (QH + 1) * t)
                turn(0)
                turn(1)
                weigh(0)
                weigh(1).then_inc(pv_psum, 1)

            def mix_out(t):
                r = rows[t]
                pe.wait_ge(mix_ready, t + 1)
                for hf in range(2):
                    for k in range(4):
                        ins = pe.transpose(ps[:, 4 + hf, P * k:P * k + r], mix[0:r, P * (4 * hf + k):P * (4 * hf + k + 1)],
                                           ident[0:r, 0:r])
                    ins.then_inc(mixT_psum, 1)
                if t == 0:
                    pe.wait_ge(ld_wout, 16)
                pe.wait_ge(o_copied, 2 * t + 2)
                for k in range(KT):
                    pe.wait_ge(mixT_ready, 2 * t + k // 4 + 1)
                    for n in range(2):
                        ins = mm(ps[0:r, 6 + n, :], mixT[:, k, 0:r], w_out_sb[:, k, 512 * n:512 * n + 512], start=(k == 0),
                                 stop=(k == KT - 1))
                ins.then_inc(out_psum, 1)

            def router(t):
                r = rows[t]
                pe.wait_ge(h2_ready, t + 1)
                for hf in range(2):
                    for k in range(4):
                        ins = pe.transpose(ps[:, 4 + hf, P * k:P * k + r], h2[0:r, P * (4 * hf + k):P * (4 * hf + k + 1)],
                                           ident[0:r, 0:r])
                    ins.then_inc(h2T_psum, 1)
                if t < PT:
                    pe.wait_ge(max_ready, t + 1)
                for k in range(KT):
                    pe.wait_ge(h2T_ready, 2 * t + k // 4 + 1)
                    ins = mm(ps[0:NE, 2, 0:r], w_router_sb[:, k, :], mixT[:, k, 0:r], start=(k == 0), stop=(k == KT - 1))
                ins.then_inc(lgT_psum, 1)
                pe.wait_ge(lgT_ready, t + 1)
                pe.transpose(ps[0:r, 3, 0:NE], lgT[:, 0:r], ident[0:NE, 0:NE]).then_inc(lg_psum, 1)

            for t in range(NTILE):
                if t:
                    attend(t)
                if t < PT:
                    score(t + 1)
                mix_out(t)
                if t < PT:
                    gla(t + 1)
                router(t)

            pe.wait_ge(routed, NTILE)
            for t in range(NTILE + 1):
                dst = ps[:, 0, NE * t:NE * t + NE]
                for i in range(t):
                    ins = mm(dst, ones_b[:], m_keep[:, i, :], start=(i == 0), stop=(i == NTILE - 1))
                if t < NTILE:
                    ins = mm(dst, before[:], m_keep[:, t, :], start=(t == 0), stop=True)
            ins.then_inc(pos_psum, 1)
            pe.wait_ge(over_made, 1)
            for i in range(2):
                ins = mm(ps[:, 1, 16 * i:16 * i + 16], ones_f[:], one_hot[0:16, i, 0:16], start=True, stop=True)
            ins.then_inc(over_psum, 1)
            pe.drain().then_inc(mixer_left, 1)
            pe.wait_ge(mixer_left, 4)

            def find(b):
                pe.wait_ge(hit_ready, b + 1)
                for t in range(NTILE):
                    ins = mm(ps[:, 6, 0:4], hit[:, t, :], slot_cols[:, t, :], start=(t == 0), stop=(t == NTILE - 1))
                ins.then_inc(list_psum, 1)

            def turn_x(b):
                pe.wait_ge(gathered, 16 * b + 16)
                for hf in range(2):
                    for k in range(4):
                        ins = pe.transpose(ps[:, 6 + hf, P * k:P * k + P], x_rows[:, P * (4 * hf + k):P * (4 * hf + k + 1)], ident[:])
                    ins.then_inc(xT_psum, 1)

            def turn_a(b):
                pe.wait_ge(a_ready, b + 1)
                for hf in range(2):
                    for k in range(4):
                        u, j = (4 * hf + k) // 2, k % 2
                        ins = pe.transpose(ps[:, 6 + hf, P * k:P * k + P], act_g[:, 2 * P * u + j:2 * P * (u + 1):2], ident[:])
                    ins.then_inc(aT_psum, 1)

            def bias(bank, n, sel, c0, s):
                for i in range(n):
                    ins = mm(ps[:, bank + i, :], sel[:], bias_parts[:, c0 + 512 * i:c0 + 512 * i + 512], start=True, stop=False)
                ins.then_inc(s, 1)

            def products(slot, hi_lo, q, outs):
                xh, xl = hi_lo
                pe.wait_ge(hi_ready, q + 1)
                for side in (xh, xl):
                    for bank, k, c, _ in outs:
                        mm(ps[:, bank, :], side[:, k, :], w_hi[:, slot, c:c + 512], start=False, stop=False)
                pe.wait_ge(lo_ready, q + 1)
                for bank, k, c, last in outs:
                    ins = mm(ps[:, bank, :], xh[:, k, :], w_lo[:, slot, c:c + 512], start=False, stop=last)
                ins.then_inc(slot_used, 1)

            def up_unit(j, q):
                products(j % RING, (xT_hi, xT_lo), q, [(n, j, 512 * n, j == UPU - 1) for n in range(4)])

            def down_unit(j, q):
                products(j % RING, (aT_hi, aT_lo), q,
                         [(4 + n, 2 * j + i, FF * i + 512 * n, j == DNU - 1 and i == 1) for i in range(2) for n in range(2)])

            pe.sem_inc(slot_used, DNU)
            find(0)
            turn_x(0)
            pe.wait_ge(sel_up_ready, 1)
            bias(0, 4, sel_up, 0, up_bias_done)
            pe.wait_ge(xT_ready, 2)
            up_unit(0, DNU)
            find(1)
            for j in range(1, UPU):
                up_unit(j, DNU + j)
            turn_x(1)
            nb = block_count(pe)
            with pe.Fori(1, nb) as b:
                q0 = UPB * b
                pe.wait_ge(sel_up_ready, b + 1)
                pe.wait_ge(up_read, b)
                bias(0, 4, sel_up, 0, up_bias_done)
                pe.wait_ge(xT_ready, 2 * b + 2)
                up_unit(0, q0)
                find(b + 1)
                for j in range(1, 4):
                    up_unit(j, q0 + j)
                pe.wait_ge(idx_ready, b + 2)
                turn_a(b - 1)
                for j in range(4, UPU):
                    up_unit(j, q0 + j)
                    pe.wait_ge(sel_dn_ready, b)
                pe.wait_ge(y_ready, b)
                bias(4, 2, sel_dn, 2 * FF, dn_bias_done)
                pe.wait_ge(aT_ready, 2 * b)
                for j in range(DNU):
                    down_unit(j, q0 + UPU + j)
                    if j == 1:
                        turn_x(b + 1)
            q0 = UPB * nb
            pe.wait_ge(xT_ready, 2 * nb + 2)
            turn_a(nb - 1)
            pe.wait_ge(sel_dn_ready, nb)
            pe.wait_ge(y_ready, nb)
            bias(4, 2, sel_dn, 2 * FF, dn_bias_done)
            pe.wait_ge(aT_ready, 2 * nb)
            for j in range(DNU):
                down_unit(j, q0 + j)


_INS = ["x_prompt", "x_sample", "state_gla", "cache_swa_k", "cache_swa_v", "meta_tokens", "rel_bias_table", "g_mix",
        "w_in", "w_a_up", "b_a", "g_gla_out", "g_swa_out", "attn_sinks", "w_out", "g_ffn", "w_router", "b_router",
        "w_up", "b_up", "w_down", "b_down", "g_final"]
_OUTS = [(1, SEQ, D), (NS, 1, D), (1, 1, GH, DK, DV), (1, 1, WIN, KVH, HD), (1, 1, WIN, KVH, HD), (1, NS, GH, DK, DV),
         (1, NS, WIN, KVH, HD), (1, NS, WIN, KVH, HD)]


def _bucket(dist):
    exact = BUCKETS // 2
    if dist < exact:
        return dist
    return min(exact + int(math.log(dist / exact) / math.log(WIN / exact) * (BUCKETS - exact)), BUCKETS - 1)


def kernel(**inputs):
    import numpy as _np
    import concourse.bacc as _bacc
    from concourse import mybir as _mybir
    from concourse.bass_utils import run_bass_kernel_spmd as _run

    nc = _bacc.Bacc("TRN2", target_bir_lowering=False, num_devices=1)
    arrays, args = {}, []
    for name in _INS:
        a = _np.ascontiguousarray(inputs[name])
        arrays[f"in_{name}_dram"] = a
        args.append(nc.dram_tensor(f"in_{name}_dram", a.shape, _mybir.dt.from_np(a.dtype), kind="ExternalInput").ap())
    hot = _np.zeros((BUCKETS, WIN), _np.float32)
    for x in range(WIN):
        hot[_bucket(WIN - 1 - x), x] = 1.0
    arrays["in_bucket_dram"] = hot
    args.append(nc.dram_tensor("in_bucket_dram", hot.shape, F32, kind="ExternalInput").ap())
    for i, shape in enumerate(_OUTS):
        args.append(nc.dram_tensor(f"out_{i}_dram", shape, F32, kind="ExternalOutput").ap())
    moe_layer(nc, *args)
    r = _run(nc, [arrays], core_ids=[0])
    return tuple(r.results[0][f"out_{i}_dram"] for i in range(len(_OUTS)))
```

```python
import math
from contextlib import ExitStack

import concourse.bass as bass
from concourse import mybir

F32 = mybir.dt.float32
F32R = mybir.dt.float32r
BF16 = mybir.dt.bfloat16
I32 = mybir.dt.int32
U32 = mybir.dt.uint32
ALU = mybir.AluOpType
ACT = mybir.ActivationFunctionType
AX = mybir.AxisListType.X

P = 128
D = 1024
KT = D // P
SEQ, META, NS = 512, 16, 8
SMALL = META + NS
PT = SEQ // P
NTILE = PT + 1
T = SMALL + SEQ
HALF = T // 2
TOK = SEQ + NS
GH, DK, DV, LOWRANK, CHUNK = 4, 64, 128, 16, 64
QH, KVH, HD, WIN = 8, 2, 64, 128
NE, TOPK, FF = 32, 4, 1024
ALPHA, LIMIT, EPS, TAU = 1.702, 7.0, 1e-6, 16.0
BUCKETS = 32
GQ, GK, GV = 0, GH * DK, 2 * GH * DK
GR = GV + GH * DV
GA = GR + GH * DV
SQ = GA + LOWRANK
SK = SQ + QH * HD
SV = SK + KVH * HD
DIN = SV + KVH * HD
MASKED = -1e30
MAXBLK = NE + TOK * TOPK // P
BLKS = MAXBLK + 2
FAR = 65536.0
UNIT = 2048
UPU, DNU, RING = 8, 4, 4
UPB = UPU + DNU
SQRT_HD = HD ** -0.5


def moe_layer(nc, x_prompt, x_sample, state_gla, cache_k, cache_v, meta, bias_tab, g_mix, w_in, w_a_up, b_a,
              g_gla, g_swa, sinks, w_out, g_ffn, w_router, b_router, w_up, b_up, w_down, b_down, g_final,
              bucket_hot, y_p, y_s, st_p, ck_p, cv_p, st_s, ck_s, cv_s):
    xn_dram = nc.dram_tensor("expert_inputs", (TOK, D), F32, kind="Internal").ap()
    x2_dram = nc.dram_tensor("residual", (TOK, D), F32, kind="Internal").ap()
    slot_dram = nc.dram_tensor("slot_outputs", (TOK * TOPK, D), F32, kind="Internal").ap()
    skew_dram = nc.dram_tensor("bias_rows", (P, QH * 3 * P), F32, kind="Internal").ap()

    rows = [SMALL] + [P] * PT
    cols = [(0, SMALL)] + [(SMALL + P * i, SMALL + P * (i + 1)) for i in range(PT)]

    with ExitStack() as ctx:
        def sem(name):
            return ctx.enter_context(nc.semaphore(name))

        base = (nc.sbuf_base + 31) // 32 * 32
        room = (nc.sbuf_usable_end - base) // 32 * 32
        ctx.enter_context(nc.sbuf_tensor("arena", [P, (room - 64) // 4], F32))

        class Region:

            def __init__(self, start, end):
                self.at, self.end = start, end

            def __call__(self, name, shape, dt=F32):
                n = math.prod(shape[1:]) * (2 if dt == BF16 else 4)
                t = nc.alloc_sbuf_tensor_at(name, list(shape), dt, offset=base + self.at)
                self.at += (n + 31) // 32 * 32
                assert self.at <= self.end, (name, self.at, self.end)
                return t

        RAW0, SPL0 = 0, UPB * UNIT * 4
        WORK0 = SPL0 + 2 * RING * UNIT * 4
        KEEP0 = WORK0 + 9 * D * 4
        END = room - 64

        keep = Region(KEEP0, END)
        ident = keep("ident", [P, P])
        slots_row = keep("slots_row", [P, P])
        bias_parts = keep("bias_parts", [P, 3 * D], BF16)
        pos_table = keep("pos_table", [P, NTILE, NE])
        slot_table = keep("slot_table", [P, NTILE, NE, 4], BF16)
        gates = keep("gates", [P, NTILE, TOPK])
        blk_expert = keep("blk_expert", [P, BLKS])
        blk_start = keep("blk_start", [P, BLKS])
        blk_row = keep("blk_row", [1, BLKS + 1], I32)
        expert_of_row = keep("expert_of_row", [P, 1])
        hit = keep("hit", [P, NTILE, P], BF16)
        sel_up = keep("sel_up", [P, P], BF16)
        sel_dn = keep("sel_dn", [P, P], BF16)
        shifted = keep("shifted", [P, NTILE])
        slot_cols = keep("slot_cols", [P, NTILE, 4], BF16)
        found = keep("found", [P, 4])
        empty = keep("empty", [P, 1])
        token_f = keep("token_f", [P, 1])
        slot_f = keep("slot_f", [P, 1])
        token_idx = keep("token_idx", [P, 1], I32)
        slot_idx = keep("slot_idx", [P, 4], I32)
        slot_tmp = keep("slot_tmp", [P, 3], I32)

        R = Region(RAW0, SPL0)
        raw = R("raw", [P, UPB, UNIT])
        R = Region(SPL0, WORK0)
        w_hi = R("w_hi", [P, RING, UNIT], F32R)
        w_lo = R("w_lo", [P, RING, UNIT], F32R)
        R = Region(WORK0, KEEP0)
        x_rows = R("x_rows", [P, D])
        xT_hi = R("xT_hi", [P, KT, P], F32R)
        xT_lo = R("xT_lo", [P, KT, P], F32R)
        aT_hi = R("aT_hi", [P, KT, P], F32R)
        aT_lo = R("aT_lo", [P, KT, P], F32R)
        act_g = R("act_g", [P, D])
        act_s = R("act_s", [P, D])
        act_l = R("act_l", [P, D])
        y_rows = R("y_rows", [P, D])
        R = Region(RAW0, RAW0 + UPU * UNIT * 4)
        g_final_bc = R("g_final_bc", [P, D])
        t_x2 = [R(f"t_x2{i}", [P, D]) for i in range(NTILE)]
        t_sq = R("t_sq", [P, D])
        t_eps = R("t_eps", [P, 1])
        t_stat = R("t_stat", [P, NTILE, 4])
        R = Region(R.at, WORK0)
        t_slots = [R(f"t_slots{i}", [P, TOPK, D]) for i in range(NTILE)]

        R = Region(RAW0, SPL0)
        w_in_sb = R("w_in_sb", [P, KT, DIN])
        x_sb = R("x_sb", [P, NTILE, D])
        R = Region(SPL0, KEEP0)
        hT = R("hT", [P, KT, T])
        sqT = R("sqT", [P, 4, T])
        skT = R("skT", [P, T])
        gla0 = R.at
        gqT = R("gqT", [P, 2, T])
        gkT = R("gkT", [P, 2, T])
        decay = R("decay", [P, 2, T])
        e_pos = R("e_pos", [P, 2, T])
        qd = R("qd", [P, 2, T])
        kd = R("kd", [P, 2, T])
        ks = R("ks", [P, 2, T])
        B = Region(gla0 + 3 * 2 * T * 4, R.at)
        skew_src = B("skew_src", [P, QH, 3 * P])
        ks_rows = R("ks_rows", [P, NTILE, 2, P])
        gv0 = R.at
        gv = R("gv", [P, NTILE, GH * DV])
        gate = R("gate", [P, NTILE, GH * DV])
        b_stage = Region(gv0, R.at)("b_stage", [3 * NE, 3 * D])
        sv = R("sv", [P, NTILE, KVH * HD])
        states = R("states", [P, NS, 2, DV])
        w_a_sb = R("w_a_sb", [LOWRANK, GH * DK])
        gaT = R("gaT", [LOWRANK, T])
        m_keep = R("m_keep", [P, NTILE, NE], BF16)
        g_mixT = R("g_mixT", [P, KT])
        g_outT = R("g_outT", [P, KT])
        b_aT = R("b_aT", [P, 2])
        b_rT = R("b_rT", [NE, 1])
        stat = R("stat", [P, 16])
        sink_bc = R("sink_bc", [P, QH])
        sink_col = R("sink_col", [QH, 1])
        row_ok = R("row_ok", [SMALL, 1])
        pidx = R("pidx", [P, 1])
        before = R("before", [P, P], BF16)
        ones_b = R("ones_b", [P, P], BF16)
        ones_f = R("ones_f", [16, P])
        same_chunk = R("same_chunk", [P, P])
        tab_sb = R("tab_sb", [BUCKETS, QH])
        hot_sb = R("hot_sb", [BUCKETS, WIN])
        bias_s = R("bias_s", [QH, WIN])
        norm = R("norm", [P, 48])
        soft = R("soft", [P, 4, QH])
        top_v = R("top_v", [P, 8])
        top_i = R("top_i", [P, 8], U32)
        top_f = R("top_f", [P, 8])
        pT_s = R("pT_s", [P, NS, QH])
        small_s = R("small_s", [QH, 4, NS])
        B = Region(SPL0, SPL0 + KT * T * 4)
        gla_state = B("gla_state", [P, 9, 2, DV])
        q_diag = B("q_diag", [P, 2, NS, SMALL])
        q_swa = B("q_swa", [P, NS, QH])
        a_gla = B("a_gla", [P, GH, P])
        lgT = B("lgT", [NE, P])
        EARLY = 1
        B = Region(RAW0 + EARLY * UNIT * 4, SPL0)
        w_out_sb = B("w_out_sb", [P, KT, D])
        bias_sb = B("bias_sb", [P, QH, 2 * P])
        probs_at = B.at
        probs = B("probs", [P, QH, 2 * P])
        pT_at = B.at
        pT = B("pT", [P, 4, 4, P])
        mix = B("mix", [P, D])
        mixT = B("mixT", [P, KT, P])
        h2_at = B.at
        h2 = B("h2", [P, D])
        g_ffn_bc = B("g_ffn_bc", [P, D])
        w_router_sb = B("w_router_sb", [P, KT, NE])
        xr = B("xr", [P, D])
        sample_at = B.at
        k_s = B("k_s", [P, NS, KVH * HD])
        v_s = B("v_s", [P, NS, KVH * HD])
        k_rows_s = B("k_rows_s", [SMALL, 2, P])
        sk_rows_s = B("sk_rows_s", [SMALL, P])
        ck_rows = B("ck_rows", [P, P])
        k_diag = Region(probs_at, pT_at)("k_diag", [SMALL, NS, 2 * P])
        B = Region(pT_at, pT_at + 2 * D * 4)
        p_s = B("p_s", [QH, NS, WIN])
        kT_s = B("kT_s", [P, NS, P])
        B = Region(h2_at, h2_at + D * 4)
        o_s = B("o_s", [QH, NS, P])
        B = Region(sample_at, sample_at + D * 4)
        one_hot = B("one_hot", [P, TOPK, NE])
        one_hot_k = B("one_hot_k", [P, TOPK, NE])
        over = B("over", [P, 4, NE])
        over_end = B("over_end", [P, 4, NE])
        zT = nc.alloc_sbuf_tensor_at("zT", [P, 2, T], F32, offset=base + gla0 + 6 * 2 * T * 4)
        z_l = nc.alloc_sbuf_tensor_at("z_l", [P, 2, T], F32, offset=base + gla0 + 3 * 2 * T * 4)
        scan_keep = nc.alloc_sbuf_tensor_at("scan_keep", [P, T], F32, offset=base + gla0 + 4 * 2 * T * 4)
        ps = ctx.enter_context(nc.psum_tensor("ps", [P, 8, 512], F32))

        ld_x = [sem(f"ld_x{t}") for t in range(NTILE)]
        ld_win = [sem(f"ld_win{k}") for k in range(KT)]
        ld_tables, ld_gmix, ld_small, ld_biases = sem("ld_tables"), sem("ld_gmix"), sem("ld_small"), sem("ld_biases")
        ld_wout, ld_sample, ld_new_rows, ld_attn = sem("ld_wout"), sem("ld_sample"), sem("ld_new_rows"), sem("ld_attn")
        ld_xr, skew_written, skew_read, o_moved = sem("ld_xr"), sem("skew_written"), sem("skew_read"), sem("o_moved")
        outputs = sem("outputs")
        consts, flanks, parts_made, scan_set = sem("consts"), sem("flanks"), sem("parts_made"), sem("scan_set")
        x_var, x_root, x_rstd, hn_ready = sem("x_var"), sem("x_root"), sem("x_rstd"), sem("hn_ready")
        hT_psum, hT_ready = sem("hT_psum"), sem("hT_ready")
        skew_psum, skew_filled, scan_cleared = sem("skew_psum"), sem("skew_filled"), sem("scan_cleared")
        colp_psum, colp_copied = sem("colp_psum"), sem("colp_copied")
        rowp_psum, gv_copied, sig_made, sv_copied, gate_made = (
            sem("rowp_psum"), sem("gv_copied"), sem("sig_made"), sem("sv_copied"), sem("gate_made"))
        soft_ready, decay_ready, exps_ready, gla_ready = sem("soft_ready"), sem("decay_ready"), sem("exps_ready"), sem("gla_ready")
        rowsT_psum, rowsT_copied, kv_psum, state_made = sem("rowsT_psum"), sem("rowsT_copied"), sem("kv_psum"), sem("state_made")
        a_psum, a_masked, o_psum, o_copied = sem("a_psum"), sem("a_masked"), sem("o_psum"), sem("o_copied")
        diags_made, outer_psum, s_state_made = sem("diags_made"), sem("outer_psum"), sem("s_state_made")
        ksT_psum, ksT_copied, s_score_psum, s_shifted, s_exp, s_probs = (
            sem("ksT_psum"), sem("ksT_copied"), sem("s_score_psum"), sem("s_shifted"), sem("s_exp"), sem("s_probs"))
        s_pT_psum, s_pT_copied, s_pv_psum, s_o_copied = sem("s_pT_psum"), sem("s_pT_copied"), sem("s_pv_psum"), sem("s_o_copied")
        score_psum, max_ready, exp_done, pT_psum, pT_copied, pv_psum, pv_copied = (
            sem("score_psum"), sem("max_ready"), sem("exp_done"), sem("pT_psum"), sem("pT_copied"), sem("pv_psum"), sem("pv_copied"))
        m_var, m_root, mix_ready, mixT_psum, mixT_ready, out_psum, x2_ready = (
            sem("m_var"), sem("m_root"), sem("mix_ready"), sem("mixT_psum"), sem("mixT_ready"), sem("out_psum"), sem("x2_ready"))
        x2_var, x2_root, h2_ready, h2_stored, x2_stored = sem("x2_var"), sem("x2_root"), sem("h2_ready"), sem("h2_stored"), sem("x2_stored")
        h2T_psum, h2T_ready, lgT_psum, lgT_ready, lg_psum, top_ready, gate_exp, routed = (
            sem("h2T_psum"), sem("h2T_ready"), sem("lgT_psum"), sem("lgT_ready"), sem("lg_psum"), sem("top_ready"), sem("gate_exp"), sem("routed"))
        pos_psum, over_made, over_psum, table_made = sem("pos_psum"), sem("over_made"), sem("over_psum"), sem("table_made")
        mixer_left = sem("mixer_left")
        rows_asked = sem("rows_asked")
        landed = [sem(f"landed{j}") for j in range(UPB)]
        slot_used = sem("slot_used")
        hi_ready, lo_ready, lo_ready_pool = sem("hi_ready"), sem("lo_ready"), sem("lo_ready_pool")
        hit_ready, list_psum, idx_ready, gathered = sem("hit_ready"), sem("list_psum"), sem("idx_ready"), sem("gathered")
        aged = sem("aged")
        xT_psum, xT_hi_ready, xT_ready = sem("xT_psum"), sem("xT_hi_ready"), sem("xT_ready")
        sel_up_ready, sel_dn_ready, up_bias_done, dn_bias_done = (
            sem("sel_up_ready"), sem("sel_dn_ready"), sem("up_bias_done"), sem("dn_bias_done"))
        up_read, g_ready, sigm_ready, a_ready = sem("up_read"), sem("g_ready"), sem("sigm_ready"), sem("a_ready")
        aT_psum, aT_hi_ready, aT_ready = sem("aT_psum"), sem("aT_hi_ready"), sem("aT_ready")
        y_ready, scattered = sem("y_ready"), sem("scattered")
        t_loaded, t_x2_loaded = [sem(f"t_loaded{t}") for t in range(NTILE)], sem("t_x2_loaded")
        t_rest_loaded, T_REST = ld_win[0:NTILE], 32
        ld_gfinal, t_summed, t_root, t_y, t_stored = sem("ld_gfinal"), sem("t_summed"), sem("t_root"), sem("t_y"), sem("t_stored")
        dve_own, act_own, pool_own = sem("dve_own"), sem("act_own"), sem("pool_own")

        def bc(ap, axis, shape):
            return ap.unsqueeze(axis).to_broadcast(list(shape))

        def head(h):
            return slice(DK * (h % 2), DK * (h % 2) + DK), h // 2

        COLP = ([("ga", GA, LOWRANK), ("gk0", GK, P), ("gk1", GK + P, P), ("gq0", GQ, P), ("gq1", GQ + P, P),
                 ("z0", 0, P), ("z1", P, P), ("sk", SK, P)] + [(f"sq{j}", SQ + j * P, P) for j in range(4)])
        NCOLP = 2 * len(COLP)
        NZ = 14

        class Own:

            def __init__(self, eng, s, start=0):
                self.eng, self.s, self.start, self.n = eng, s, start, 0

            def step(self, ins):
                ins.then_inc(self.s, 1)
                self.n += 1
                return ins

            def settle(self):
                self.eng.wait_ge(self.s, self.start + self.n)

            def do(self, ins):
                self.step(ins)
                self.settle()

        NCONST = 16 + 2 * NTILE
        NB_ROW = blk_row[0:1, BLKS:BLKS + 1]

        def up_end(b):
            return UPB if isinstance(b, int) and b == 0 else UPB * b + UPU

        POOLED = (0, 4, 9)
        BY_DVE = UPB - len(POOLED)

        def wait_lo(e, b, i, ends=False):
            if ends:
                e.wait_ge(lo_ready, BY_DVE * b + i + 1 - (len(POOLED) if isinstance(b, int) else 0))
            elif i in POOLED:
                e.wait_ge(lo_ready_pool, len(POOLED) * b + POOLED.index(i) + 1)
            else:
                e.wait_ge(lo_ready, BY_DVE * b + i + 1 - len([p for p in POOLED if p < i]))

        def block_count(e):
            return e.value_load(NB_ROW, min_val=NE - 2, max_val=MAXBLK - 2) + 2

        def expert(e, b):
            if isinstance(b, int):
                return b
            return e.value_load(blk_row[0:1, bass.ds(b, 1)], min_val=0, max_val=NE - 1)

        block = ctx.enter_context(nc.Block())

        @block.gpsimd
        def _(pool):
            own = Own(pool, pool_own)
            made = Own(pool, consts)
            pool.memset(ident[:], 0.0).then_inc(pool_own, 1)
            pool.memset(same_chunk[:], 1.0).then_inc(pool_own, 1)
            pool.memset(before[:], 1.0).then_inc(pool_own, 1)
            pool.memset(row_ok[:], 1.0).then_inc(pool_own, 1)
            own.n = 4
            own.settle()
            made.do(pool.affine_select(out=ident[:], in_=ident[:], compare_op=ALU.not_equal, fill=1.0, base=0,
                               pattern=[[-1, P]], channel_multiplier=1))
            pool.memset(skew_src[:, :, 0:P], MASKED).then_inc(flanks, 1)
            pool.memset(skew_src[:, :, 2 * P:3 * P], MASKED).then_inc(flanks, 1)
            made.do(pool.affine_select(out=before[:], in_=before[:], compare_op=ALU.is_gt, fill=0.0, base=0,
                               pattern=[[1, P]], channel_multiplier=-1))
            own.do(pool.affine_select(out=same_chunk[:], in_=same_chunk[:], compare_op=ALU.is_ge, fill=0.0, base=0,
                                      pattern=[[1, P]], channel_multiplier=-1))
            made.do(pool.memset(same_chunk[0:CHUNK, CHUNK:P], 0.0))
            made.do(pool.affine_select(out=row_ok[:], in_=row_ok[:], compare_op=ALU.is_ge, fill=0.0, base=-META,
                               pattern=[[0, 1]], channel_multiplier=1))
            made.do(pool.memset(ones_b[:], 1.0))
            made.do(pool.memset(ones_f[:], 1.0))
            made.do(pool.iota(slots_row[:], pattern=[[1, P]], base=0, channel_multiplier=0,
                      allow_small_or_imprecise_dtypes=True))
            made.do(pool.iota(pidx[:], pattern=[[0, 1]], base=0, channel_multiplier=1,
                      allow_small_or_imprecise_dtypes=True))
            for j in range(3):
                made.do(pool.iota(expert_of_row[NE * j:NE * j + NE, :], pattern=[[0, 1]], base=0, channel_multiplier=1,
                          allow_small_or_imprecise_dtypes=True))
            made.do(pool.memset(expert_of_row[3 * NE:P, :], -1.0))
            made.do(pool.memset(m_keep[:], 0.0))
            assert made.n == NCONST - 2 * NTILE - 3
            for t in range(NTILE):
                first = SEQ - META if t == 0 else P * (t - 1)
                made.do(pool.iota(slot_table[:, t, :, 0], pattern=[[0, NE]], base=0, channel_multiplier=1,
                          allow_small_or_imprecise_dtypes=True))
                made.do(pool.memset(slot_table[:, t, :, 1], first / 16.0))
            made.do(pool.memset(slot_table[:, :, :, 2], 0.0))
            made.do(pool.memset(slot_table[:, :, :, 3], 1.0))
            made.do(pool.memset(gates[:], 0.0))
            own.do(pool.memset(bias_parts[3 * NE:P, :], 0.0))
            pool.wait_ge(skew_written, 16)
            own.do(pool.memset(scan_keep[:], 1.0))
            pool.memset(scan_keep[:, 0:1], 0.0).then_inc(scan_set, 1)
            pool.memset(scan_keep[:, META:SMALL], 0.0).then_inc(scan_set, 1)
            pool.memset(scan_keep[:, SMALL:T:CHUNK], 0.0).then_inc(scan_set, 1)

            pool.drain().then_inc(mixer_left, 1)
            pool.wait_ge(mixer_left, 4)
            pool.wait_ge(h2_stored, 16 * NTILE)
            own.do(pool.memset(x_rows[:], 0.0))
            own.do(pool.memset(y_rows[:], 0.0))
            pool.iota(slot_idx[:], pattern=[[0, 4]], base=0, channel_multiplier=1).then_inc(table_made, 1)
            last_token = pool.to_reg(TOK - 1)
            last_slot = pool.to_reg(TOK * TOPK - 1)

            def gather(b):
                pool.wait_ge(idx_ready, b + 1)
                if not (isinstance(b, int) and b == 0):
                    pool.wait_ge(xT_psum, 2 * b)
                pool.sem_inc(rows_asked, 1)
                pool.indirect_dma_start(x_rows[:], None, xn_dram[:, :],
                                        bass.IndirectOffsetOnAxis(ap=token_idx[:, 0:1], axis=0),
                                        bounds_check=last_token, oob_is_err=False).then_inc(gathered, 16)

            def scatter(col, rows_ready, made):
                pool.wait_ge(y_ready, rows_ready)
                pool.wait_ge(aged, made)
                pool.sem_inc(rows_asked, 1)
                pool.indirect_dma_start(slot_dram[:, :], bass.IndirectOffsetOnAxis(ap=slot_idx[:, col:col + 1], axis=0),
                                        y_rows[:], None, bounds_check=last_slot,
                                        oob_is_err=False).then_inc(scattered, 16)

            def lo(slot, unit, q):
                pool.wait_ge(hi_ready, q + 1)
                pool.tensor_tensor(w_lo[:, slot, :], raw[:, unit, :], w_hi[:, slot, :].bitcast(F32),
                                   ALU.subtract).then_inc(lo_ready_pool, 1)

            pool.sem_inc(lo_ready_pool, len(POOLED))
            gather(0)
            gather(1)
            nb = block_count(pool)
            with pool.Fori(1, nb) as b:
                q0 = UPB * b
                lo(POOLED[0] % RING, POOLED[0], q0 + POOLED[0])
                scatter(3, b, b + 1)
                lo(POOLED[1] % RING, POOLED[1], q0 + POOLED[1])
                gather(b + 1)
                lo(POOLED[2] % RING, POOLED[2], q0 + POOLED[2])
            scatter(3, nb, nb + 1)
            scatter(2, nb + 1, nb + 1)

        @block.sync
        def _(sp):
            def load_up(e, j):
                src = w_up[0, bass.ds(e, 1), P * j:P * j + P, :] if not isinstance(e, int) else w_up[0, e:e + 1, P * j:P * j + P, :]
                sp.dma_start(raw[:, j, :], src.rearrange("a p n -> p (a n)")).then_inc(landed[j], 16)
            sp.dma_start(x_sb[0:META, 0, :], meta).then_inc(ld_x[0], 16)
            sp.dma_start(x_sb[META:SMALL, 0, :], x_sample.rearrange("b s d -> (b s) d")).then_inc(ld_x[0], 16)
            for i in range(PT):
                sp.dma_start(x_sb[:, 1 + i, :], x_prompt[0, P * i:P * i + P, :]).then_inc(ld_x[1 + i], 16)
            for k in range(KT):
                sp.dma_start(w_in_sb[:, k, :], w_in[0, P * k:P * k + P, :]).then_inc(ld_win[k], 16)
            for j in range(3):
                sp.dma_start(b_stage[NE * j:NE * j + NE, 0:2 * FF], b_up[0]).then_inc(ld_biases, 16)
                sp.dma_start(b_stage[NE * j:NE * j + NE, 2 * FF:3 * FF], b_down[0]).then_inc(ld_biases, 16)
            sp.dma_start(states[:], state_gla[0].rearrange("b (r h) k v -> (h k) b r v", h=2)).then_inc(ld_sample, 16)
            sp.wait_ge(rowp_psum, 3 * NTILE)
            load_up(0, 0)
            for src, dst in ((cache_k, k_s), (cache_v, v_s)):
                sp.dma_start(dst[0:WIN - 1, :, :], src[0, :, 1:WIN].rearrange("b j g d -> j b (g d)")).then_inc(ld_sample, 16)
            sp.dma_start(w_out_sb[:], w_out[0].rearrange("(k p) n -> p k n", p=P)).then_inc(ld_wout, 16)
            sp.dma_start(g_ffn_bc[:], g_ffn[0:1, :].to_broadcast([P, D])).then_inc(ld_attn, 16)
            sp.dma_start(w_router_sb[:], w_router[0].rearrange("(k p) n -> p k n", p=P)).then_inc(ld_attn, 16)
            sp.wait_ge(skew_written, 16)
            skewed = bass.AP(tensor=skew_dram.tensor, offset=P - 1, ap=[[QH * 3 * P - 1, P], [3 * P, QH], [1, 2 * P]])
            sp.dma_start(bias_sb[:], skewed).then_inc(skew_read, 16)
            sp.wait_ge(rowsT_copied, 1)
            sp.dma_start(k_s[WIN - 1:WIN, :, :], sk_rows_s[META:SMALL, :]).then_inc(ld_new_rows, 16)
            sp.wait_ge(sv_copied, NTILE)
            sp.dma_start(v_s[WIN - 1:WIN, :, :], sv[META:SMALL, 0, :]).then_inc(ld_new_rows, 16)
            sp.wait_ge(ld_sample, 48)
            sp.wait_ge(ld_new_rows, 32)
            sp.dma_start(ck_s[0].rearrange("b j g d -> j b (g d)"), k_s[:]).then_inc(outputs, 16)
            sp.dma_start(cv_s[0].rearrange("b j g d -> j b (g d)"), v_s[:]).then_inc(outputs, 16)
            sp.dma_start(ck_p[0, 0].rearrange("j g d -> j (g d)"), ck_rows[:]).then_inc(outputs, 16)
            sp.dma_start(cv_p[0, 0].rearrange("j g d -> j (g d)"), sv[:, NTILE - 1, :]).then_inc(outputs, 16)
            sp.dma_start(xr[0:META, :], meta).then_inc(ld_xr, 16)
            sp.dma_start(xr[META:SMALL, :], x_sample.rearrange("b s d -> (b s) d")).then_inc(ld_xr, 16)
            sp.wait_ge(s_state_made, NS)
            sp.dma_start(st_s[0].rearrange("b (r h) k v -> (h k) b r v", h=2), states[:]).then_inc(outputs, 16)
            sp.wait_ge(state_made, 9)
            sp.dma_start(st_p[0, 0].rearrange("(r h) k v -> (h k) r v", h=2), gla_state[:, 8]).then_inc(outputs, 16)
            sp.wait_ge(s_o_copied, 1)
            for g in range(KVH):
                for hh in range(4):
                    h = 4 * g + hh
                    sp.dma_start(mix[META:SMALL, D // 2 + HD * h:D // 2 + HD * h + HD],
                                 o_s[h:h + 1, :, HD * g:HD * g + HD]).then_inc(o_moved, 16)
            for t in range(NTILE):
                n, lo = (NS, META) if t == 0 else (P, 0)
                first = SEQ if t == 0 else P * (t - 1)
                if t == PT:
                    sp.wait_ge(pv_psum, PT)
                    for j in range(5, UPU):
                        load_up(0, j)
                    sp.wait_ge(out_psum, NTILE)
                    for j in range(1, 5):
                        load_up(0, j)
                sp.wait_ge(x2_ready, t + 1)
                sp.dma_start(x2_dram[first:first + n, :], xr[lo:lo + n, :]).then_inc(x2_stored, 16)
                sp.wait_ge(h2_ready, t + 1)
                sp.dma_start(xn_dram[first:first + n, :], h2[lo:lo + n, :]).then_inc(h2_stored, 16)
                if t < PT:
                    sp.wait_ge(x2_stored, 16 * (t + 1))
                    sp.dma_start(xr[:], x_prompt[0, P * t:P * t + P, :]).then_inc(ld_xr, 16)
            sp.wait_ge(x2_stored, 16 * NTILE)
            sp.wait_ge(h2_stored, 16 * NTILE)
            sp.wait_ge(outputs, 6 * 16)
            sp.wait_ge(mixer_left, 4)

            def load_down(e, j):
                src = w_down[0, e:e + 1, 2 * P * j:2 * P * (j + 1), :] if isinstance(e, int) else w_down[0, bass.ds(e, 1), 2 * P * j:2 * P * (j + 1), :]
                sp.dma_start(raw[:, UPU + j, :], src.rearrange("a (p r) n -> p (a r n)", r=2)).then_inc(landed[UPU + j], 16)

            for j in range(2):
                load_down(0, j)
            sp.wait_ge(gathered, 16)
            for j in range(2, DNU):
                load_down(0, j)
            sp.wait_ge(table_made, 2)
            nb = block_count(sp)
            for j in range(UPU):
                wait_lo(sp, 0, DNU + j, ends=True)
                load_up(1, j)
            with sp.Fori(2, nb) as b:
                e_up, e_dn = expert(sp, b), expert(sp, b - 1)
                for j in range(UPU):
                    wait_lo(sp, b - 1, j)
                    load_up(e_up, j)
                for j in range(DNU):
                    wait_lo(sp, b - 1, UPU + j)
                    load_down(e_dn, j)
            e_dn = expert(sp, nb - 1)
            for j in range(DNU):
                wait_lo(sp, nb - 1, UPU + j)
                load_down(e_dn, j)
            sp.wait_ge(slot_used, UPB * nb)
            sp.dma_start(g_final_bc[:], g_final.rearrange("(a n) -> a n", a=1).to_broadcast([P, D])).then_inc(ld_gfinal, 16)
            parts = [(NS, META, SEQ)] + [(P, 0, P * i) for i in range(PT)]
            for t, (n, first_row, token) in enumerate(parts):
                sp.dma_start(t_x2[t][first_row:first_row + n, :], x2_dram[token:token + n, :]).then_inc(t_x2_loaded, 16)
            sp.wait_ge(scattered, 16 * nb + 16)
            for t, (n, first_row, token) in enumerate(parts):
                slots = slot_dram[TOPK * token:TOPK * (token + n), :].rearrange("(p k) n -> p k n", k=TOPK)
                sp.dma_start(t_slots[t][first_row:first_row + n, 0:2, :], slots[:, 0:2, :]).then_inc(t_loaded[t], 16)
                sp.dma_start(t_slots[t][first_row:first_row + n, 2:4, :], slots[:, 2:4, :]).then_inc(t_rest_loaded[t], 16)
            for t, (n, first_row, token) in enumerate(parts):
                dst = y_s.rearrange("b s d -> (b s) d") if t == 0 else y_p[0, token:token + n, :]
                sp.wait_ge(t_y, t + 1)
                sp.dma_start(dst, t_x2[t][first_row:first_row + n, :]).then_inc(t_stored, 16)
            sp.wait_ge(t_stored, 16 * NTILE)

        @block.scalar
        def _(act):
            own = Own(act, act_own)
            with nc.allow_non_contiguous_dma(reason="columns of small tables"):
                act.dma_start(tab_sb[:], bias_tab).then_inc(ld_tables, 16)
                act.dma_start(hot_sb[:], bucket_hot).then_inc(ld_tables, 16)

                act.dma_start(g_mixT[:], g_mix[0].rearrange("(k p) -> p k", p=P)).then_inc(ld_gmix, 16)
                act.dma_start(w_a_sb[:], w_a_up[0]).then_inc(ld_small, 16)
                act.dma_start(b_aT[:], b_a[0].rearrange("(k p) -> p k", p=P)).then_inc(ld_small, 16)
                act.dma_start(g_outT[:, 4:8], g_swa[0].rearrange("(k p) -> p k", p=P)).then_inc(ld_small, 16)
                for h in range(GH):
                    act.dma_start(g_outT[:, h:h + 1], g_gla[0].rearrange("(p a) -> p a", a=1)).then_inc(ld_small, 16)
                act.dma_start(b_rT[:], b_router[0].rearrange("(p a) -> p a", a=1)).then_inc(ld_small, 16)
                act.dma_start(sink_col[:], sinks[0].rearrange("(p a) -> p a", a=1)).then_inc(ld_small, 16)
                act.dma_start(sink_bc[:], sinks[0:1, :].to_broadcast([P, QH])).then_inc(ld_small, 16)
            for t in range(NTILE):
                r = rows[t]
                act.wait_ge(x_var, t + 1)
                act.activation(stat[0:r, 5 + t:6 + t], stat[0:r, t:t + 1], ACT.Sqrt).then_inc(x_root, 1)
                act.wait_ge(x_rstd, t + 1)
                act.activation(x_sb[0:r, t, :], x_sb[0:r, t, :], ACT.Copy, scale=stat[0:r, 10 + t:11 + t]).then_inc(hn_ready, 1)
            act.wait_ge(skew_filled, 1)
            act.wait_ge(flanks, 2)
            act.dma_start(skew_dram, skew_src[:, :, :]).then_inc(skew_written, 16)
            act.wait_ge(ld_small, 10 * 16)

            def copy_colp(n):
                name, _, w = COLP[n // 2]
                half = slice(HALF * (n % 2), HALF * (n % 2) + HALF)
                src = ps[0:w, n % 4, 0:HALF]
                act.wait_ge(colp_psum, n + 1)
                if name[:2] == "sq":
                    for i in range(2):
                        g, j = divmod(2 * int(name[2]) + i, 4)
                        ins = act.activation(sqT[HD * g:HD * g + HD, j, half], ps[HD * i:HD * i + HD, n % 4, 0:HALF],
                                             ACT.Copy, scale=SQRT_HD)
                    ins.then_inc(colp_copied, 1)
                    return
                if n == 10:
                    act.wait_ge(skew_written, 16)
                dst, func, kw = {
                    "ga": (gaT[:, half], ACT.Copy, {}), "gk": (gkT[:, int(name[-1]) if name[-1] in "01" else 0, half], ACT.Copy, {}),
                    "gq": (gqT[:, int(name[-1]) if name[-1] in "01" else 0, half], ACT.Copy, {"scale": DK ** -0.5}),
                    "z0": (zT[:, 0, half], ACT.Identity, {"bias": b_aT[:, 0:1]}),
                    "z1": (zT[:, 1, half], ACT.Identity, {"bias": b_aT[:, 1:2]}),
                    "sk": (skT[:, half], ACT.Copy, {}),
                }[name[:2]]
                act.activation(dst, src, func, **kw).then_inc(colp_copied, 1)

            for n in range(NZ):
                copy_colp(n)
            act.wait_ge(colp_copied, NZ)
            own.do(act.activation(z_l[:], zT[:], ACT.Abs))
            own.do(act.activation(z_l[:], z_l[:], ACT.Exp, scale=-1.0))
            act.activation(z_l[:], z_l[:], ACT.Ln, bias=1.0).then_inc(soft_ready, 1)
            for n in range(NZ, NCOLP):
                copy_colp(n)
            act.wait_ge(decay_ready, 1)
            act.activation(e_pos[:], decay[:], ACT.Exp, scale=1.0 / TAU).then_inc(exps_ready, 1)
            act.activation(kd[:], decay[:], ACT.Exp, scale=-1.0 / TAU).then_inc(exps_ready, 1)
            act.activation(ks[:], ks[:], ACT.Exp, scale=1.0 / TAU).then_inc(exps_ready, 1)
            for t in range(NTILE):
                r = rows[t]
                act.wait_ge(rowp_psum, 3 * t + 1)
                if t == 0:
                    act.wait_ge(parts_made, 1)
                act.activation(gv[0:r, t, :], ps[0:r, 4 + t % 2, :], ACT.Copy).then_inc(gv_copied, 1)
                act.wait_ge(rowp_psum, 3 * t + 2)
                act.activation(gate[0:r, t, :], ps[0:r, 6 + t % 2, :], ACT.Sigmoid).then_inc(sig_made, 1)
                act.wait_ge(rowp_psum, 3 * t + 3)
                act.activation(sv[0:r, t, :], ps[0:r, t % 2, 0:P], ACT.Copy).then_inc(sv_copied, 1)

            for hf in range(2):
                act.wait_ge(ksT_psum, hf + 1)
                act.activation(kT_s[:, 4 * hf:4 * hf + 4, :], ps[:, 4 + hf, :].rearrange("p (b j) -> p b j", b=4),
                               ACT.Copy).then_inc(ksT_copied, 1)
            act.wait_ge(s_shifted, 1)
            act.activation(p_s[:], p_s[:], ACT.Exp).then_inc(s_exp, 1)
            act.activation(small_s[:, 2, :], small_s[:, 1, :], ACT.Exp).then_inc(s_exp, 1)

            def roots(t):
                r = rows[t]
                act.wait_ge(m_var, t + 1)
                act.activation(norm[0:r, 8:13], norm[0:r, 0:5], ACT.Sqrt).then_inc(m_root, 1)

            def softmax(t):
                act.wait_ge(max_ready, t)
                w0 = P - META if t == 1 else 0
                for h in range(QH):
                    act.activation(probs[:, h, w0:2 * P], probs[:, h, w0:2 * P], ACT.Exp, bias=soft[:, 1, h:h + 1],
                                   accum_out=soft[:, 2, h:h + 1]).then_inc(exp_done, 1)
                act.activation(soft[:, 3, :], soft[:, 3, :], ACT.Exp).then_inc(exp_done, 1)

            def move_pT(t):
                for q in range(4):
                    g, part = q // 2, q % 2
                    n = META if t == 1 and part == 0 else P
                    act.wait_ge(pT_psum, 4 * (t - 1) + q + 1)
                    act.activation(pT[0:n, q, :, :], ps[0:n, 4 + part, :].rearrange("p (h q) -> p h q", h=4),
                                   ACT.Copy).then_inc(pT_copied, 1)

            def x2_rms(t):
                r = rows[t]
                act.wait_ge(x2_var, t + 1)
                act.activation(norm[0:r, 25:26], norm[0:r, 24:25], ACT.Sqrt).then_inc(x2_root, 1)

            def finish(t):
                r = rows[t]
                for hf in range(2):
                    act.wait_ge(h2T_psum, 2 * t + hf + 1)
                    act.activation(mixT[:, 4 * hf:4 * hf + 4, 0:r],
                                   ps[:, 4 + hf, :].rearrange("p (k q) -> p k q", k=4)[:, :, 0:r], ACT.Copy).then_inc(h2T_ready, 1)
                act.wait_ge(lgT_psum, t + 1)
                act.activation(lgT[:, 0:r], ps[0:NE, 6, 0:r], ACT.Identity, bias=b_rT[:]).then_inc(lgT_ready, 1)
                act.wait_ge(top_ready, t + 1)
                act.activation(norm[0:r, 32:36], top_v[0:r, 0:TOPK], ACT.Exp, bias=norm[0:r, 40:41],
                               accum_out=norm[0:r, 41:42]).then_inc(gate_exp, 1)

            roots(0)
            for t in range(NTILE):
                if t < PT:
                    softmax(t + 1)
                x2_rms(t)
                if t < PT:
                    move_pT(t + 1)
                    roots(t + 1)
                finish(t)
            act.drain().then_inc(mixer_left, 1)
            act.wait_ge(mixer_left, 4)

            def hi(slot, unit, q, land):
                act.wait_ge(landed[unit], land)
                act.wait_ge(slot_used, q - RING + 1)
                act.activation(w_hi[:, slot, :], raw[:, unit, :], ACT.Copy).then_inc(hi_ready, 1)

            def x_hi(b):
                for hf in range(2):
                    act.wait_ge(xT_psum, 2 * b + hf + 1)
                    act.activation(xT_hi[:, 4 * hf:4 * hf + 4, :], ps[:, 6 + hf, :].rearrange("p (k q) -> p k q", k=4),
                                   ACT.Copy).then_inc(xT_hi_ready, 1)

            def a_hi(b):
                for hf in range(2):
                    act.wait_ge(aT_psum, 2 * b + hf + 1)
                    act.activation(aT_hi[:, 4 * hf:4 * hf + 4, :], ps[:, 6 + hf, :].rearrange("p (k q) -> p k q", k=4),
                                   ACT.Copy).then_inc(aT_hi_ready, 1)

            def sigmoid(b):
                act.wait_ge(g_ready, b + 1)
                act.activation(act_s[:], act_g[:], ACT.Sigmoid, scale=ALPHA).then_inc(sigm_ready, 1)

            def y_out(used):
                act.wait_ge(slot_used, used)
                act.activation(y_rows[:], ps[:, 4:6, :].rearrange("p a n -> p (a n)"), ACT.Copy).then_inc(y_ready, 1)

            act.sem_inc(y_ready, 1)
            act.sem_inc(hi_ready, DNU)
            x_hi(0)
            for j in range(UPU):
                hi(j % RING, j, DNU + j, 16)
            sigmoid(0)
            x_hi(1)
            nb = block_count(act)
            with act.Fori(1, nb) as b:
                q0 = UPB * b
                for j in range(4):
                    hi(j % RING, j, q0 + j, 16 * b + 16)
                with act.If(b > 1):
                    act.wait_ge(aged, b + 1)
                    y_out(UPB * b)
                for j in range(4, 6):
                    hi(j % RING, j, q0 + j, 16 * b + 16)
                a_hi(b - 1)
                for j in range(6, UPU):
                    hi(j % RING, j, q0 + j, 16 * b + 16)
                for j in range(DNU):
                    hi(j % RING, UPU + j, q0 + UPU + j, 16 * b)
                    if j == 2:
                        sigmoid(b)
                x_hi(b + 1)
            q0 = UPB * nb
            act.wait_ge(aged, nb + 1)
            y_out(UPB * nb)
            a_hi(nb - 1)
            for j in range(DNU):
                hi(j % RING, UPU + j, q0 + j, 16 * nb)
            act.wait_ge(scattered, 16 * nb)
            y_out(UPB * nb + DNU)
            for t in range(NTILE):
                r = rows[t]
                act.wait_ge(t_summed, t + 1)
                own.do(act.activation(t_sq[0:r, :], t_x2[t][0:r, :], ACT.Square, accum_out=t_stat[0:r, t, 0:1]))
                act.activation(t_stat[0:r, t, 1:2], t_stat[0:r, t, 0:1], ACT.Sqrt, scale=1.0 / D, bias=t_eps[0:r, :]).then_inc(t_root, 1)

        @block.vector
        def _(dve):
            own = Own(dve, dve_own)
            step, settle, do = own.step, own.settle, own.do
            junk = gate[:, 3:5, :].rearrange("p a n -> p (a n)")
            for t in range(NTILE):
                r = rows[t]
                dve.wait_ge(ld_x[t], 32 if t == 0 else 16)
                do(dve.tensor_tensor_reduce(junk[0:r, :], x_sb[0:r, t, :], x_sb[0:r, t, :], 1.0, 0.0, ALU.mult, ALU.add,
                                            stat[0:r, t:t + 1]))
                do(dve.tensor_scalar(stat[0:r, t:t + 1], stat[0:r, t:t + 1], 1.0 / D, EPS, ALU.mult, ALU.add))
                dve.sem_inc(x_var, 1)
                dve.wait_ge(x_root, t + 1)
                dve.reciprocal(stat[0:r, 10 + t:11 + t], stat[0:r, 5 + t:6 + t]).then_inc(x_rstd, 1)
            dve.wait_ge(skew_psum, 1)
            for i in range(2):
                do(dve.tensor_copy(skew_src[:, 4 * i:4 * i + 4, P:2 * P], ps[:, i, :].rearrange("p (h x) -> p h x", h=4)))
            do(dve.tensor_copy(bias_s[:], ps[0:QH, 2, 0:WIN]))
            dve.sem_inc(skew_filled, 1)
            dve.wait_ge(ld_gmix, 16)
            for t in range(NTILE):
                a, z = cols[t]
                for hf in range(2):
                    dve.wait_ge(hT_psum, 2 * t + hf + 1)
                    dve.tensor_tensor(hT[:, 4 * hf:4 * hf + 4, a:z],
                                      ps[:, 4 + (2 * t + hf) % 4, :].rearrange("p (k q) -> p k q", k=4)[:, :, 0:z - a],
                                      bc(g_mixT[:, 4 * hf:4 * hf + 4], 2, [P, 4, z - a]), ALU.mult).then_inc(hT_ready, 1)
            dve.wait_ge(ld_biases, 6 * 16)
            do(dve.tensor_copy(bias_parts[0:3 * NE, :], b_stage[:]))
            do(dve.tensor_tensor(b_stage[:], b_stage[:], bias_parts[0:3 * NE, :], ALU.subtract))
            for j in (1, 2):
                step(dve.tensor_copy(bias_parts[NE * j:NE * j + NE, :], b_stage[NE * j:NE * j + NE, :]))
            settle()
            two = slice(2 * NE, 3 * NE)
            do(dve.tensor_tensor(b_stage[two, :], b_stage[two, :], bias_parts[two, :], ALU.subtract))
            dve.tensor_copy(bias_parts[two, :], b_stage[two, :]).then_inc(parts_made, 1)
            dve.wait_ge(soft_ready, 1)
            do(dve.scalar_tensor_tensor(z_l[:], zT[:], 0.0, z_l[:], ALU.min, ALU.subtract))
            dve.wait_ge(scan_set, 3)
            for r in range(2):
                step(dve.tensor_tensor_scan(decay[:, r, :], scan_keep[:], z_l[:, r, :], 0.0, ALU.mult, ALU.add))
            settle()
            for r in range(2):
                step(dve.tensor_tensor(ks[:, r, 0:META], decay[:, r, META - 1:META].to_broadcast([P, META]),
                                       decay[:, r, 0:META], ALU.subtract))
                d = decay[:, r, SMALL:T].rearrange("p (c s) -> p c s", s=CHUNK)
                step(dve.tensor_tensor(ks[:, r, SMALL:T].rearrange("p (c s) -> p c s", s=CHUNK),
                                       d[:, :, CHUNK - 1:CHUNK].to_broadcast([P, SEQ // CHUNK, CHUNK]), d, ALU.subtract))
            step(dve.memset(ks[:, :, META:SMALL], 0.0))
            settle()
            dve.sem_inc(decay_ready, 1)
            dve.wait_ge(exps_ready, 3)
            step(dve.tensor_tensor(qd[:], gqT[:], e_pos[:], ALU.mult))
            step(dve.tensor_tensor(kd[:], gkT[:], kd[:], ALU.mult))
            step(dve.tensor_tensor(ks[:], gkT[:], ks[:], ALU.mult))
            settle()
            dve.sem_inc(gla_ready, 1)
            for t in range(NTILE):
                r = rows[t]
                dve.wait_ge(sig_made, t + 1)
                dve.tensor_tensor(gate[0:r, t, :], ps[0:r, 6 + t % 2, :], gate[0:r, t, :], ALU.mult).then_inc(gate_made, 1)
            dve.wait_ge(consts, NCONST)
            dve.wait_ge(rowsT_psum, 1)
            step(dve.tensor_copy(k_rows_s[:], ps[0:SMALL, 0, 0:2 * P].rearrange("p (r x) -> p r x", r=2)))
            step(dve.tensor_copy(sk_rows_s[:], ps[0:SMALL, 0, 2 * P:3 * P]))
            step(dve.tensor_copy(ck_rows[:], ps[:, 0, 3 * P:4 * P]))
            step(dve.tensor_copy(ks_rows[0:META, 0], ps[0:META, 1, 0:2 * P].rearrange("p (r x) -> p r x", r=2)))
            step(dve.tensor_copy(ks_rows[:, 1:5], ps[:, 2:4, :].rearrange("p a (t r x) -> p (a t) r x", t=2, r=2)))
            settle()
            dve.sem_inc(rowsT_copied, 1)
            step(dve.memset(q_diag[:], 0.0))
            step(dve.memset(q_swa[:], 0.0))
            for b in range(NS):
                step(dve.tensor_scalar(k_diag[:, b, :], k_rows_s[:].rearrange("p r x -> p (r x)"),
                                       ident[0:SMALL, META + b:META + b + 1], None, ALU.mult))
            settle()
            for r in range(2):
                flat = q_diag[:, r].rearrange("p b c -> p (b c)")
                step(dve.tensor_copy(flat[:, META:META + (SMALL + 1) * (NS - 1) + 1:SMALL + 1], gqT[:, r, META:SMALL]))
            for g in range(KVH):
                half = slice(HD * g, HD * g + HD)
                step(dve.tensor_copy(q_swa[half, :, 4 * g:4 * g + 4],
                                     sqT[half, :, META:SMALL].rearrange("p j b -> p b j")))
            settle()
            dve.sem_inc(diags_made, 1)
            for c in range(9):
                dve.wait_ge(kv_psum, c + 1)
                src = ps[:, 4 + c % 4, 0:256].rearrange("p (r v) -> p r v", r=2)
                if c == 0:
                    step(dve.tensor_copy(gla_state[:, 0], src))
                else:
                    end = SMALL + CHUNK * c - 1
                    for r in range(2):
                        step(dve.scalar_tensor_tensor(gla_state[:, c, r, :], gla_state[:, c - 1, r, :],
                                                      e_pos[:, r, end:end + 1], src[:, r, :], ALU.mult, ALU.add))
                settle()
                dve.sem_inc(state_made, 1)
            dve.wait_ge(ld_sample, 48)
            for b in range(NS):
                dve.wait_ge(outer_psum, b // 2 + 1)
                for r in range(2):
                    src = ps[:, b // 2, 256 * (b % 2) + P * r:256 * (b % 2) + P * r + P]
                    step(dve.scalar_tensor_tensor(states[:, b, r, :], states[:, b, r, :],
                                                  e_pos[:, r, META + b:META + b + 1], src, ALU.mult, ALU.add))
                settle()
                dve.sem_inc(s_state_made, 1)
            dve.wait_ge(s_score_psum, 1)
            do(dve.tensor_tensor(p_s[:], ps[0:QH, 0:2, :].rearrange("p a (b j) -> p (a b) j", b=4),
                                 bc(bias_s[:], 1, [QH, NS, WIN]), ALU.add))
            do(dve.tensor_reduce(small_s[:, 0, :], p_s[:], AX, ALU.max))
            do(dve.tensor_scalar(small_s[:, 0, :], small_s[:, 0, :], sink_col[:], None, ALU.max))
            step(dve.tensor_scalar(small_s[:, 1, :], small_s[:, 0, :], -1.0, sink_col[:], ALU.mult, ALU.add))
            step(dve.tensor_tensor(p_s[:], p_s[:], bc(small_s[:, 0, :], 2, [QH, NS, WIN]), ALU.subtract))
            settle()
            dve.sem_inc(s_shifted, 1)
            dve.wait_ge(s_exp, 2)
            do(dve.tensor_reduce(small_s[:, 3, :], p_s[:], AX, ALU.add))
            do(dve.tensor_tensor(small_s[:, 3, :], small_s[:, 3, :], small_s[:, 2, :], ALU.add))
            do(dve.reciprocal(small_s[:, 3, :], small_s[:, 3, :]))
            dve.tensor_tensor(p_s[:], p_s[:], bc(small_s[:, 3, :], 2, [QH, NS, WIN]), ALU.mult).then_inc(s_probs, 1)
            dve.wait_ge(s_pT_psum, 1)
            dve.tensor_copy(pT_s[:], ps[:, 2, 0:NS * QH].rearrange("p (b h) -> p b h", b=NS)).then_inc(s_pT_copied, 1)
            dve.wait_ge(s_pv_psum, 1)
            do(dve.memset(mix[0:SMALL, D // 2:D], 0.0))
            dve.tensor_copy(o_s[:], ps[0:QH, 0:2, :].rearrange("p a (b x) -> p (a b) x", b=4)).then_inc(s_o_copied, 1)

            def mask_gla(t):
                dve.wait_ge(a_psum, t)
                for i in range(2):
                    dve.tensor_tensor(a_gla[:, i:GH:2, :], ps[:, 2 + i, 0:256].rearrange("p (h q) -> p h q", h=2),
                                      bc(same_chunk[:], 1, [P, 2, P]), ALU.mult).then_inc(a_masked, 1)

            def take_gla(t):
                r = rows[t]
                bank = 2 if t else 6
                dve.wait_ge(o_psum, t + 1)
                if t:
                    dve.wait_ge(mixT_psum, 2 * t)
                for i in range(2):
                    dve.tensor_copy(mix[0:r, 0:D // 2].rearrange("p (h v) -> p h v", h=GH)[:, i:GH:2, :],
                                    ps[0:r, bank + i, 256:512].rearrange("p (h v) -> p h v", h=2)).then_inc(o_copied, 1)

            def scores(t):
                w0 = P - META if t == 1 else 0
                if t == 1:
                    dve.wait_ge(skew_read, 16)
                dve.wait_ge(score_psum, t)
                if t == 1:
                    dve.wait_ge(s_pT_copied, 1)
                for i in range(4):
                    step(dve.tensor_tensor(probs[:, 2 * i:2 * i + 2, w0:2 * P],
                                           ps[:, i, :].rearrange("p (h j) -> p h j", h=2)[:, :, w0:2 * P],
                                           bias_sb[:, 2 * i:2 * i + 2, w0:2 * P], ALU.add))
                settle()
                do(dve.tensor_reduce(soft[:, 0, :], probs[:, :, w0:2 * P], AX, ALU.max))
                do(dve.tensor_tensor(soft[:, 0, :], soft[:, 0, :], sink_bc[:], ALU.max))
                step(dve.tensor_scalar(soft[:, 1, :], soft[:, 0, :], -1.0, None, ALU.mult))
                step(dve.tensor_tensor(soft[:, 3, :], sink_bc[:], soft[:, 0, :], ALU.subtract))
                settle()
                dve.sem_inc(max_ready, 1)

            def take_attention(t):
                dve.wait_ge(exp_done, (QH + 1) * t)
                do(dve.tensor_tensor(soft[:, 0, :], soft[:, 2, :], soft[:, 3, :], ALU.add))
                do(dve.reciprocal(soft[:, 0, :], soft[:, 0, :]))
                dve.wait_ge(pv_psum, t)
                for g in range(KVH):
                    step(dve.tensor_tensor(
                        mix[:, D // 2 + 256 * g:D // 2 + 256 * g + 256].rearrange("p (h x) -> p h x", h=4),
                        ps[:, g, :].rearrange("p (h x) -> p h x", h=4)[:, :, HD * g:HD * g + HD],
                        bc(soft[:, 0, 4 * g:4 * g + 4], 2, [P, 4, HD]), ALU.mult))
                settle()
                dve.sem_inc(pv_copied, 1)

            def gla_variance(t):
                r = rows[t]
                scratch = a_gla[0:r].rearrange("p h q -> p (h q)")
                dve.wait_ge(o_copied, 2 * t + 2)
                do(dve.tensor_tensor(scratch, mix[0:r, 0:D // 2], mix[0:r, 0:D // 2], ALU.mult))
                do(dve.tensor_reduce(norm[0:r, 0:4], scratch.rearrange("p (h v) -> p h v", h=GH), AX, ALU.add))

            def variances(t):
                r = rows[t]
                scratch = a_gla[0:r].rearrange("p h q -> p (h q)")
                do(dve.tensor_tensor_reduce(scratch, mix[0:r, D // 2:D], mix[0:r, D // 2:D], 1.0, 0.0, ALU.mult, ALU.add,
                                            norm[0:r, 4:5]))
                step(dve.tensor_scalar(norm[0:r, 0:4], norm[0:r, 0:4], 1.0 / DV, EPS, ALU.mult, ALU.add))
                step(dve.tensor_scalar(norm[0:r, 4:5], norm[0:r, 4:5], 1.0 / (QH * HD), EPS, ALU.mult, ALU.add))
                settle()
                dve.sem_inc(m_var, 1)

            def make_mix(t):
                r = rows[t]
                dve.wait_ge(m_root, t + 1)
                do(dve.reciprocal(norm[0:r, 16:21], norm[0:r, 8:13]))
                for h in range(GH):
                    m = mix[0:r, DV * h:DV * h + DV]
                    step(dve.scalar_tensor_tensor(m, m, norm[0:r, 16 + h:17 + h], gate[0:r, t, DV * h:DV * h + DV],
                                                  ALU.mult, ALU.mult))
                m = mix[0:r, D // 2:D]
                step(dve.tensor_scalar(m, m, norm[0:r, 20:21], None, ALU.mult))
                settle()
                dve.sem_inc(mix_ready, 1)

            def take_mixT(t):
                r = rows[t]
                for hf in range(2):
                    dve.wait_ge(mixT_psum, 2 * t + hf + 1)
                    if t:
                        dve.wait_ge(lgT_psum, t)
                    dve.tensor_tensor(mixT[:, 4 * hf:4 * hf + 4, 0:r],
                                      ps[:, 4 + hf, :].rearrange("p (k q) -> p k q", k=4)[:, :, 0:r],
                                      bc(g_outT[:, 4 * hf:4 * hf + 4], 2, [P, 4, r]), ALU.mult).then_inc(mixT_ready, 1)

            def residual(t):
                r = rows[t]
                dve.wait_ge(ld_xr, 16 * (t + 2))
                dve.wait_ge(out_psum, t + 1)
                do(dve.tensor_tensor(xr[0:r, :], ps[0:r, 6:8, :].rearrange("p a n -> p (a n)"), xr[0:r, :], ALU.add))
                dve.sem_inc(x2_ready, 1)
                if t:
                    dve.wait_ge(h2_stored, 16 * t)
                do(dve.tensor_tensor_reduce(h2[0:r, :], xr[0:r, :], xr[0:r, :], 1.0, 0.0, ALU.mult, ALU.add, norm[0:r, 24:25]))
                do(dve.tensor_scalar(norm[0:r, 24:25], norm[0:r, 24:25], 1.0 / D, EPS, ALU.mult, ALU.add))
                dve.sem_inc(x2_var, 1)
                dve.wait_ge(x2_root, t + 1)
                do(dve.reciprocal(norm[0:r, 26:27], norm[0:r, 25:26]))
                if t == 0:
                    dve.wait_ge(ld_attn, 32)
                dve.scalar_tensor_tensor(h2[0:r, :], xr[0:r, :], norm[0:r, 26:27], g_ffn_bc[0:r, :], ALU.mult,
                                         ALU.mult).then_inc(h2_ready, 1)

            def choose(t):
                r = rows[t]
                dve.wait_ge(lg_psum, t + 1)
                lg = ps[0:r, 7, 0:NE]
                do(dve.max(top_v[0:r, :], lg))
                step(dve.max_index(top_i[0:r, :], top_v[0:r, :], lg))
                step(dve.tensor_scalar(norm[0:r, 40:41], top_v[0:r, 0:1], -1.0, None, ALU.mult))
                settle()
                dve.sem_inc(top_ready, 1)

            def route(t):
                r = rows[t]
                do(dve.tensor_copy(top_f[0:r, :], top_i[0:r, :]))
                do(dve.tensor_tensor(one_hot[0:r], bc(slots_row[0:r, 0:NE], 1, [r, TOPK, NE]),
                                     bc(top_f[0:r, 0:TOPK], 2, [r, TOPK, NE]), ALU.is_equal))
                if t == 0:
                    do(dve.tensor_scalar(one_hot[0:r], one_hot[0:r], row_ok[:], None, ALU.mult))
                step(dve.tensor_tensor(one_hot_k[0:r], one_hot[0:r], bc(slots_row[0:r, 0:TOPK], 2, [r, TOPK, NE]), ALU.mult))
                with nc.allow_low_precision(reason="zeros and ones"):
                    step(dve.tensor_reduce(m_keep[0:r, t, :], one_hot[0:r].rearrange("p k e -> p e k"), AX, ALU.add))
                settle()
                with nc.allow_low_precision(reason="integers up to three"):
                    step(dve.tensor_reduce(slot_table[0:r, t, :, 2], one_hot_k[0:r].rearrange("p k e -> p e k"), AX, ALU.add))
                dve.wait_ge(gate_exp, t + 1)
                do(dve.reciprocal(norm[0:r, 42:43], norm[0:r, 41:42]))
                step(dve.tensor_scalar(gates[0:r, t, :], norm[0:r, 32:36], norm[0:r, 42:43], None, ALU.mult))
                settle()
                dve.sem_inc(routed, 1)

            take_gla(0)
            gla_variance(0)
            dve.wait_ge(o_moved, 16 * QH)
            variances(0)
            make_mix(0)
            take_mixT(0)
            scores(1)
            mask_gla(1)
            for t in range(NTILE):
                residual(t)
                if t < PT:
                    take_gla(t + 1)
                    gla_variance(t + 1)
                    take_attention(t + 1)
                    variances(t + 1)
                    make_mix(t + 1)
                choose(t)
                if t < PT:
                    take_mixT(t + 1)
                if t + 2 < NTILE:
                    scores(t + 2)
                route(t)
                if t + 2 < NTILE:
                    mask_gla(t + 2)

            dve.wait_ge(pos_psum, 1)
            do(dve.scalar_tensor_tensor(pos_table[:], ps[:, 0, 0:NTILE * NE].rearrange("p (t e) -> p t e", t=NTILE), 1.0,
                                        m_keep[:], ALU.add, ALU.mult))
            do(dve.tensor_scalar(pos_table[:], pos_table[:], -1.0, None, ALU.add))
            count = ps[:, 0, NTILE * NE:(NTILE + 1) * NE]
            for m in range(4):
                step(dve.tensor_scalar(over[:, m, :], count, float(P * (m + 1)), None, ALU.is_gt))
            settle()
            flat, flat_end = over[:].rearrange("p m e -> p (m e)"), over_end[:].rearrange("p m e -> p (m e)")
            ones_row = one_hot_k[:].rearrange("p k e -> p (k e)")
            do(dve.memset(ones_row, 1.0))
            do(dve.tensor_tensor_scan(flat_end, ones_row, flat, 0.0, ALU.mult, ALU.add))
            step(dve.tensor_scalar(norm[:, 0:1], flat_end[:, 4 * NE - 1:4 * NE], float(NE - 2), None, ALU.add))
            settle()
            do(dve.tensor_tensor(flat_end, flat_end, flat, ALU.subtract))
            do(dve.scalar_tensor_tensor(flat, flat_end, pidx[:], flat, ALU.is_equal, ALU.mult))
            do(dve.tensor_tensor(over_end[:], over[:], bc(slots_row[:, 0:NE], 1, [P, 4, NE]), ALU.mult))
            step(dve.tensor_reduce(norm[:, 1:2], flat_end, AX, ALU.add))
            step(dve.tensor_reduce(norm[:, 4:8], over[:], AX, ALU.add))
            settle()
            do(dve.tensor_tensor(norm[:, 4:8], norm[:, 4:8], slots_row[:, 1:5], ALU.mult))
            do(dve.tensor_reduce(norm[:, 2:3], norm[:, 4:8], AX, ALU.add))
            do(dve.tensor_scalar(norm[:, 2:3], norm[:, 2:3], float(P), None, ALU.mult))
            for i in range(2):
                step(dve.tensor_scalar(one_hot[0:16, i, 0:16], ident[0:16, 0:16], norm[0:16, 1 + i:2 + i], None, ALU.mult))
            settle()
            dve.sem_inc(over_made, 1)
            step(dve.memset(blk_expert[:], 0.0))
            step(dve.memset(blk_start[:], 0.0))
            settle()
            step(dve.tensor_copy(blk_expert[:, 0:NE], slots_row[:, 0:NE]))
            dve.wait_ge(over_psum, 1)
            step(dve.tensor_copy(blk_expert[:, NE:NE + 16], ps[:, 1, 0:16]))
            step(dve.tensor_copy(blk_start[:, NE:NE + 16], ps[:, 1, 16:32]))
            settle()
            step(dve.tensor_copy(blk_row[0:1, 0:BLKS], blk_expert[0:1, :]))
            step(dve.tensor_copy(blk_row[0:1, BLKS:BLKS + 1], norm[0:1, 0:1]))
            settle()
            dve.sem_inc(table_made, 1)
            dve.sem_inc(mixer_left, 1)
            dve.wait_ge(mixer_left, 4)
            dve.wait_ge(table_made, 2)
            OWN0 = own.n

            def find_slots(o, b):
                e = expert(dve, b)
                col = slice(e, e + 1) if isinstance(e, int) else bass.ds(e, 1)
                bcol = slice(b, b + 1) if isinstance(b, int) else bass.ds(b, 1)
                o.step(dve.tensor_scalar(shifted[:].unsqueeze(2), pos_table[:, :, col], blk_start[:, bcol], None, ALU.subtract))
                o.step(dve.tensor_copy(slot_cols[:].unsqueeze(2), slot_table[:, :, col, :]))
                o.settle()
                dve.tensor_tensor(hit[:], bc(slots_row[:], 1, [P, NTILE, P]), bc(shifted[:], 2, [P, NTILE, P]),
                                  ALU.is_equal).then_inc(hit_ready, 1)

            def indices(o, b):
                dve.wait_ge(list_psum, b + 1)
                o.do(dve.tensor_copy(found[:], ps[:, 6, 0:4]))
                o.step(dve.tensor_scalar(empty[:], found[:, 3:4], -FAR, FAR, ALU.mult, ALU.add))
                o.step(dve.scalar_tensor_tensor(token_f[:], found[:, 1:2], 16.0, found[:, 0:1], ALU.mult, ALU.add))
                o.settle()
                o.step(dve.scalar_tensor_tensor(slot_f[:], token_f[:], float(TOPK), found[:, 2:3], ALU.mult, ALU.add))
                o.step(dve.tensor_tensor(token_idx[:], token_f[:], empty[:], ALU.add))
                o.settle()
                dve.tensor_tensor(slot_idx[:, 0:1], slot_f[:], empty[:], ALU.add).then_inc(idx_ready, 1)

            def age_indices(o, made):
                dve.wait_ge(idx_ready, made)
                o.do(dve.tensor_copy(slot_tmp[:], slot_idx[:, 0:3]))
                dve.tensor_copy(slot_idx[:, 1:4], slot_tmp[:]).then_inc(aged, 1)
                dve.wait_ge(aged, made)

            def select(dst, b, s):
                bcol = slice(b, b + 1) if isinstance(b, int) else bass.ds(b, 1)
                dve.tensor_tensor(dst[:], expert_of_row[:].to_broadcast([P, P]), blk_expert[:, bcol].to_broadcast([P, P]),
                                  ALU.is_equal).then_inc(s, 1)

            def lo(slot, unit, q):
                dve.wait_ge(hi_ready, q + 1)
                ins = dve.tensor_tensor(w_lo[:, slot, :], raw[:, unit, :], w_hi[:, slot, :].bitcast(F32), ALU.subtract)
                ins.then_inc(lo_ready, 1)

            def x_lo(b):
                for hf in range(2):
                    dve.wait_ge(xT_hi_ready, 2 * b + hf + 1)
                    dve.tensor_tensor(xT_lo[:, 4 * hf:4 * hf + 4, :], ps[:, 6 + hf, :].rearrange("p (k q) -> p k q", k=4),
                                      xT_hi[:, 4 * hf:4 * hf + 4, :].bitcast(F32), ALU.subtract).then_inc(xT_ready, 1)

            def a_lo(b):
                for hf in range(2):
                    dve.wait_ge(aT_hi_ready, 2 * b + hf + 1)
                    dve.tensor_tensor(aT_lo[:, 4 * hf:4 * hf + 4, :], ps[:, 6 + hf, :].rearrange("p (k q) -> p k q", k=4),
                                      aT_hi[:, 4 * hf:4 * hf + 4, :].bitcast(F32), ALU.subtract).then_inc(aT_ready, 1)

            def clamp(b):
                dve.wait_ge(slot_used, up_end(b))
                dve.tensor_scalar(act_g[:], ps[:, 0:2, :].rearrange("p a n -> p (a n)"), LIMIT, None, ALU.min).then_inc(g_ready, 1)
                dve.tensor_scalar(act_l[:], ps[:, 2:4, :].rearrange("p a n -> p (a n)"), LIMIT, -LIMIT, ALU.min,
                                  ALU.max).then_inc(up_read, 1)

            def swiglu(o, b):
                dve.wait_ge(sigm_ready, b + 1)
                o.do(dve.tensor_tensor(act_s[:], act_g[:], act_s[:], ALU.mult))
                dve.wait_ge(up_read, b + 1)
                dve.scalar_tensor_tensor(act_g[:], act_l[:], 1.0, act_s[:], ALU.add, ALU.mult).then_inc(a_ready, 1)

            dve.sem_inc(lo_ready, DNU - len(POOLED))
            find_slots(own, 0)
            indices(own, 0)
            age_indices(own, 1)
            select(sel_up, 0, sel_up_ready)
            x_lo(0)
            find_slots(own, 1)
            for j in range(4):
                lo(j % RING, j, DNU + j)
            indices(own, 1)
            for j in range(4, UPU):
                lo(j % RING, j, DNU + j)
            dve.wait_ge(up_bias_done, 1)
            select(sel_up, 1, sel_up_ready)
            select(sel_dn, 0, sel_dn_ready)
            clamp(0)
            swiglu(own, 0)
            x_lo(1)
            age_indices(own, 2)
            before_loop = own.n
            nb = block_count(dve)
            with dve.Fori(1, nb) as b:
                STEPS = 9
                o = Own(dve, dve_own, b * STEPS + (before_loop - STEPS))
                q0 = UPB * b
                def los(*places):
                    for i in places:
                        if i not in POOLED:
                            lo(i % RING, i, q0 + i)

                los(0, 1)
                find_slots(o, b + 1)
                los(2, 3, 4)
                indices(o, b + 1)
                los(5)
                dve.wait_ge(up_bias_done, b + 1)
                select(sel_up, b + 1, sel_up_ready)
                los(6)
                a_lo(b - 1)
                los(7, 8, 9, 10)
                clamp(b)
                los(11)
                swiglu(o, b)
                x_lo(b + 1)
                dve.wait_ge(dn_bias_done, b)
                select(sel_dn, b, sel_dn_ready)
                dve.wait_ge(scattered, 16 * b)
                age_indices(o, b + 2)
                assert o.n == STEPS, o.n
            q0 = UPB * nb
            a_lo(nb - 1)
            for j in range(DNU):
                lo(j % RING, UPU + j, q0 + j)
            own = Own(dve, dve_own, nb * STEPS + (before_loop - STEPS))
            step, do, settle = own.step, own.do, own.settle
            dve.wait_ge(slot_used, UPB * nb)
            step(dve.memset(t_slots[0][0:META, :, :], 0.0))
            step(dve.memset(t_x2[0][0:META, :], 0.0))
            step(dve.memset(t_eps[:], EPS))
            settle()

            def last_norm(t):
                r = rows[t]
                dve.wait_ge(t_root, t + 1)
                do(dve.reciprocal(t_stat[0:r, t, 2:3], t_stat[0:r, t, 1:2]))
                dve.wait_ge(ld_gfinal, 16)
                dve.scalar_tensor_tensor(t_x2[t][0:r, :], t_x2[t][0:r, :], t_stat[0:r, t, 2:3], g_final_bc[0:r, :], ALU.mult,
                                         ALU.mult).then_inc(t_y, 1)

            for t in range(NTILE):
                r = rows[t]
                x2, y4 = t_x2[t], t_slots[t]
                dve.wait_ge(t_x2_loaded, 16 * NTILE)
                dve.wait_ge(t_loaded[t], 16)
                for k in range(TOPK):
                    if k == 2:
                        dve.wait_ge(t_rest_loaded[t], T_REST)
                    do(dve.scalar_tensor_tensor(x2[0:r, :], y4[0:r, k, :], gates[0:r, t, k:k + 1], x2[0:r, :], ALU.mult, ALU.add))
                dve.sem_inc(t_summed, 1)
                if t:
                    last_norm(t - 1)
            last_norm(NTILE - 1)

        @block.tensor
        def _(pe):
            mm = nc.tensor.matmul
            pe.wait_ge(ld_tables, 32)
            for h in range(QH):
                mm(ps[:, h // 4, P * (h % 4):P * (h % 4) + P], tab_sb[:, h:h + 1].to_broadcast([BUCKETS, P]), hot_sb[:],
                   start=True, stop=True)
            mm(ps[0:QH, 2, 0:WIN], tab_sb[:], hot_sb[:], start=True, stop=True).then_inc(skew_psum, 1)
            pe.wait_ge(consts, 1)
            for t in range(NTILE):
                r = rows[t]
                pe.wait_ge(hn_ready, t + 1)
                for hf in range(2):
                    n = 2 * t + hf
                    if n >= 4:
                        pe.wait_ge(hT_ready, n - 3)
                    for k in range(4):
                        ins = pe.transpose(ps[:, 4 + n % 4, P * k:P * k + r], x_sb[0:r, t, P * (4 * hf + k):P * (4 * hf + k + 1)],
                                           ident[0:r, 0:r])
                    ins.then_inc(hT_psum, 1)
            pe.wait_ge(hT_ready, 2 * NTILE)
            pe.wait_ge(skew_filled, 1)
            def column_product(n, k):
                _, c0, w = COLP[n // 2]
                return mm(ps[0:w, n % 4, 0:HALF], w_in_sb[:, k, c0:c0 + w], hT[:, k, HALF * (n % 2):HALF * (n % 2) + HALF],
                          start=(k == 0), stop=(k == KT - 1))

            for k in range(KT):
                pe.wait_ge(ld_win[k], 16)
                for n in range(4):
                    ins = column_product(n, k)
                    if k == KT - 1:
                        ins.then_inc(colp_psum, 1)
            for n in range(4, NCOLP):
                name, c0, w = COLP[n // 2]
                half = slice(HALF * (n % 2), HALF * (n % 2) + HALF)
                dst = ps[0:w, n % 4, 0:HALF]
                pe.wait_ge(colp_copied, n - 3)
                if name[0] == "z":
                    if n == 10:
                        pe.wait_ge(ld_small, 10 * 16)
                    mm(dst, w_a_sb[:, c0:c0 + P], gaT[:, half], start=True, stop=True).then_inc(colp_psum, 1)
                    continue
                for k in range(KT):
                    ins = column_product(n, k)
                ins.then_inc(colp_psum, 1)
            for t in range(NTILE):
                a, z = cols[t]
                r = z - a
                for bank, c0, w, freed in ((4 + t % 2, GV, GH * DV, gv_copied), (6 + t % 2, GR, GH * DV, gate_made),
                                           (t % 2, SV, P, sv_copied)):
                    if t >= 2:
                        pe.wait_ge(freed, t - 1)
                    elif w == P:
                        pe.wait_ge(colp_copied, NCOLP)
                    for k in range(KT):
                        ins = mm(ps[0:r, bank, 0:w], hT[:, k, a:z], w_in_sb[:, k, c0:c0 + w], start=(k == 0), stop=(k == KT - 1))
                    ins.then_inc(rowp_psum, 1)
            pe.wait_ge(gla_ready, 1)
            pe.wait_ge(sv_copied, NTILE)
            pe.wait_ge(gv_copied, NTILE)
            pe.wait_ge(gate_made, NTILE)
            for r in range(2):
                pe.transpose(ps[0:SMALL, 0, P * r:P * r + P], gkT[:, r, 0:SMALL], ident[:])
            pe.transpose(ps[0:SMALL, 0, 2 * P:3 * P], skT[:, 0:SMALL], ident[:])
            pe.transpose(ps[:, 0, 3 * P:4 * P], skT[:, T - WIN:T], ident[:])
            for r in range(2):
                pe.transpose(ps[0:META, 1, P * r:P * r + P], ks[:, r, 0:META], ident[:])
            for i in range(PT):
                for r in range(2):
                    ins = pe.transpose(ps[:, 2 + i // 2, 256 * (i % 2) + P * r:256 * (i % 2) + P * r + P],
                                       ks[:, r, SMALL + P * i:SMALL + P * i + P], ident[:])
            ins.then_inc(rowsT_psum, 1)
            pe.wait_ge(rowsT_copied, 1)
            for c in range(9):
                if c >= 4:
                    pe.wait_ge(state_made, c - 3)
                t, r0, n = (0, 0, META) if c == 0 else ((c + 1) // 2, CHUNK * ((c - 1) % 2), CHUNK)
                for h in range(GH):
                    part, pair = head(h)
                    ins = mm(ps[part, 4 + c % 4, DV * pair:DV * pair + DV], ks_rows[r0:r0 + n, t, pair, part],
                             gv[r0:r0 + n, t, DV * h:DV * h + DV], start=True, stop=True)
                ins.then_inc(kv_psum, 1)
            pe.wait_ge(diags_made, 1)
            for b in range(NS):
                for h in range(GH):
                    part, pair = head(h)
                    at = 256 * (b % 2) + DV * pair
                    ins = mm(ps[part, b // 2, at:at + DV], k_diag[:, b, DK * h:DK * h + DK], gv[0:SMALL, 0, DV * h:DV * h + DV],
                             start=True, stop=True)
                if b % 2:
                    ins.then_inc(outer_psum, 1)
            pe.wait_ge(ld_sample, 48)
            pe.wait_ge(ld_new_rows, 32)
            pe.wait_ge(state_made, 9)
            for hf in range(2):
                for i in range(4):
                    ins = pe.transpose(ps[:, 4 + hf, P * i:P * i + P], k_s[:, 4 * hf + i, :], ident[:])
                ins.then_inc(ksT_psum, 1)
            pe.wait_ge(s_state_made, NS)
            pe.wait_ge(ksT_copied, 2)
            for b in range(NS):
                ins = mm(ps[0:QH, b // 4, P * (b % 4):P * (b % 4) + P], q_swa[:, b, :], kT_s[:, b, :], start=True, stop=True)
            ins.then_inc(s_score_psum, 1)
            pe.wait_ge(state_made, 9)
            for h in range(GH):
                part, pair = head(h)
                for b in range(NS):
                    ins = mm(ps[0:SMALL, 6 + h % 2, 256 + DV * pair:256 + DV * pair + DV], q_diag[part, pair, b, :], states[part, b, pair, :],
                             start=(b == 0), stop=(b == NS - 1))
            ins.then_inc(o_psum, 1)
            pe.wait_ge(s_probs, 1)
            for b in range(NS):
                ins = pe.transpose(ps[:, 2, QH * b:QH * b + QH], p_s[:, b, :], ident[0:QH, 0:QH])
            ins.then_inc(s_pT_psum, 1)
            pe.wait_ge(s_pT_copied, 1)
            for b in range(NS):
                ins = mm(ps[0:QH, b // 4, P * (b % 4):P * (b % 4) + P], pT_s[:, b, :], v_s[:, b, :], start=True, stop=True)
            ins.then_inc(s_pv_psum, 1)

            def score(t):
                if t == 1:
                    pe.wait_ge(s_o_copied, 1)
                else:
                    pe.wait_ge(pv_copied, t - 1)
                    pe.wait_ge(o_copied, 2 * t)
                a, z = cols[t]
                for h in range(QH):
                    g = h // 4
                    half = slice(HD * g, HD * g + HD)
                    q = sqT[half, h % 4, a:z]
                    dst = ps[:, h // 2, 256 * (h % 2):256 * (h % 2) + 256]
                    if t == 1:
                        mm(dst[:, P - META:P], q, skT[half, 0:META], start=True, stop=True)
                        ins = mm(dst[:, P:2 * P], q, skT[half, a:z], start=True, stop=True)
                    else:
                        ins = mm(dst, q, skT[half, a - P:z], start=True, stop=True)
                ins.then_inc(score_psum, 1)

            def gla_weights(t):
                pe.wait_ge(max_ready, t)
                a, z = cols[t]
                for h in range(GH):
                    part, pair = head(h)
                    ins = mm(ps[:, 2 + h % 2, P * pair:P * pair + P], kd[part, pair, a:z], qd[part, pair, a:z], start=True, stop=True)
                ins.then_inc(a_psum, 1)

            def gla(t):
                a, z = cols[t]
                pe.wait_ge(a_masked, 2 * t)
                for h in range(GH):
                    part, pair = head(h)
                    o_at = slice(256 + DV * pair, 256 + DV * pair + DV)
                    mm(ps[:, 2 + h % 2, o_at], a_gla[:, h, :], gv[:, t, DV * h:DV * h + DV], start=True, stop=False,
                       skip_group_check=True)
                    for c in range(2):
                        ins = mm(ps[CHUNK * c:CHUNK * c + CHUNK, 2 + h % 2, o_at],
                                 qd[part, pair, a + CHUNK * c:a + CHUNK * c + CHUNK], gla_state[part, 2 * (t - 1) + c, pair, :],
                                 start=False, stop=True, skip_group_check=True)
                ins.then_inc(o_psum, 1)

            def attend(t):
                def turn(g):
                    for part in range(2):
                        q = 4 * (t - 1) + 2 * g + part
                        c0, n = (P - META, META) if t == 1 and part == 0 else (P * part, P)
                        if g:
                            pe.wait_ge(pT_copied, q - 1)
                        for i in range(4):
                            ins = pe.transpose(ps[0:n, 4 + part, P * i:P * i + P], probs[:, 4 * g + i, c0:c0 + n], ident[:])
                        ins.then_inc(pT_psum, 1)

                def weigh(g):
                    pe.wait_ge(pT_copied, 4 * (t - 1) + 2 * g + 2)
                    n = META if t == 1 else P
                    for i in range(4):
                        dst = ps[:, g, P * i:P * i + P]
                        mm(dst, pT[0:n, 2 * g, i, :], sv[0:n, t - 1, :], start=True, stop=False)
                        ins = mm(dst, pT[:, 2 * g + 1, i, :], sv[:, t, :], start=False, stop=True)
                    return ins

                pe.wait_ge(exp_done, (QH + 1) * t)
                turn(0)
                turn(1)
                weigh(0)
                weigh(1).then_inc(pv_psum, 1)

            def mix_out(t):
                r = rows[t]
                pe.wait_ge(mix_ready, t + 1)
                for hf in range(2):
                    for k in range(4):
                        ins = pe.transpose(ps[:, 4 + hf, P * k:P * k + r], mix[0:r, P * (4 * hf + k):P * (4 * hf + k + 1)],
                                           ident[0:r, 0:r])
                    ins.then_inc(mixT_psum, 1)
                if t == 0:
                    pe.wait_ge(ld_wout, 16)
                    pe.wait_ge(o_copied, 2)
                else:
                    pe.wait_ge(top_ready, t)
                for k in range(KT):
                    if k == 5 and t < PT:
                        gla_weights(t + 1)
                    pe.wait_ge(mixT_ready, 2 * t + k // 4 + 1)
                    for n in range(2):
                        ins = mm(ps[0:r, 6 + n, :], mixT[:, k, 0:r], w_out_sb[:, k, 512 * n:512 * n + 512], start=(k == 0),
                                 stop=(k == KT - 1))
                ins.then_inc(out_psum, 1)

            def turn_h2(t):
                r = rows[t]
                pe.wait_ge(h2_ready, t + 1)
                for hf in range(2):
                    for k in range(4):
                        ins = pe.transpose(ps[:, 4 + hf, P * k:P * k + r], h2[0:r, P * (4 * hf + k):P * (4 * hf + k + 1)],
                                           ident[0:r, 0:r])
                    ins.then_inc(h2T_psum, 1)

            def router(t):
                r = rows[t]
                for k in range(KT):
                    pe.wait_ge(h2T_ready, 2 * t + k // 4 + 1)
                    ins = mm(ps[0:NE, 6, 0:r], w_router_sb[:, k, :], mixT[:, k, 0:r], start=(k == 0), stop=(k == KT - 1))
                ins.then_inc(lgT_psum, 1)
                pe.wait_ge(lgT_ready, t + 1)
                pe.transpose(ps[0:r, 7, 0:NE], lgT[:, 0:r], ident[0:NE, 0:NE]).then_inc(lg_psum, 1)

            score(1)
            for t in range(NTILE):
                mix_out(t)
                if t < PT:
                    gla(t + 1)
                    attend(t + 1)
                turn_h2(t)
                if t + 2 < NTILE:
                    score(t + 2)
                router(t)

            pe.wait_ge(routed, NTILE)
            for t in range(NTILE + 1):
                dst = ps[:, 0, NE * t:NE * t + NE]
                for i in range(t):
                    ins = mm(dst, ones_b[:], m_keep[:, i, :], start=(i == 0), stop=(i == NTILE - 1))
                if t < NTILE:
                    ins = mm(dst, before[:], m_keep[:, t, :], start=(t == 0), stop=True)
            ins.then_inc(pos_psum, 1)
            pe.wait_ge(over_made, 1)
            for i in range(2):
                ins = mm(ps[:, 1, 16 * i:16 * i + 16], ones_f[:], one_hot[0:16, i, 0:16], start=True, stop=True)
            ins.then_inc(over_psum, 1)
            pe.drain().then_inc(mixer_left, 1)
            pe.wait_ge(mixer_left, 4)

            def find(b):
                pe.wait_ge(hit_ready, b + 1)
                for t in range(NTILE):
                    ins = mm(ps[:, 6, 0:4], hit[:, t, :], slot_cols[:, t, :], start=(t == 0), stop=(t == NTILE - 1))
                ins.then_inc(list_psum, 1)

            def turn_x(b):
                pe.wait_ge(gathered, 16 * b + 16)
                for hf in range(2):
                    for k in range(4):
                        ins = pe.transpose(ps[:, 6 + hf, P * k:P * k + P], x_rows[:, P * (4 * hf + k):P * (4 * hf + k + 1)], ident[:])
                    ins.then_inc(xT_psum, 1)

            def turn_a(b):
                pe.wait_ge(a_ready, b + 1)
                for hf in range(2):
                    for k in range(4):
                        u, j = (4 * hf + k) // 2, k % 2
                        ins = pe.transpose(ps[:, 6 + hf, P * k:P * k + P], act_g[:, 2 * P * u + j:2 * P * (u + 1):2], ident[:])
                    ins.then_inc(aT_psum, 1)

            def bias(bank, n, sel, c0, s):
                for i in range(n):
                    ins = mm(ps[:, bank + i, :], sel[:], bias_parts[:, c0 + 512 * i:c0 + 512 * i + 512], start=True, stop=False)
                ins.then_inc(s, 1)

            def products(slot, hi_lo, q, outs, lo_place):
                xh, xl = hi_lo
                pe.wait_ge(hi_ready, q + 1)
                for side in (xh, xl):
                    for bank, k, c, _ in outs:
                        mm(ps[:, bank, :], side[:, k, :], w_hi[:, slot, c:c + 512], start=False, stop=False)
                wait_lo(pe, *lo_place)
                for bank, k, c, last in outs:
                    ins = mm(ps[:, bank, :], xh[:, k, :], w_lo[:, slot, c:c + 512], start=False, stop=last)
                ins.then_inc(slot_used, 1)

            def up_unit(j, q, lo_place):
                products(j % RING, (xT_hi, xT_lo), q, [(n, j, 512 * n, j == UPU - 1) for n in range(4)], lo_place)

            def down_unit(j, q, lo_place):
                products(j % RING, (aT_hi, aT_lo), q,
                         [(4 + n, 2 * j + i, FF * i + 512 * n, j == DNU - 1 and i == 1) for i in range(2) for n in range(2)], lo_place)

            pe.sem_inc(slot_used, DNU)
            find(0)
            turn_x(0)
            pe.wait_ge(sel_up_ready, 1)
            bias(0, 4, sel_up, 0, up_bias_done)
            pe.wait_ge(xT_ready, 2)
            up_unit(0, DNU, (0, DNU, True))
            find(1)
            for j in range(1, UPU):
                up_unit(j, DNU + j, (0, DNU + j, True))
            turn_x(1)
            nb = block_count(pe)
            with pe.Fori(1, nb) as b:
                q0 = UPB * b
                pe.wait_ge(sel_up_ready, b + 1)
                pe.wait_ge(up_read, b)
                bias(0, 4, sel_up, 0, up_bias_done)
                pe.wait_ge(xT_ready, 2 * b + 2)
                up_unit(0, q0, (b, 0))
                find(b + 1)
                for j in range(1, 4):
                    up_unit(j, q0 + j, (b, j))
                pe.wait_ge(idx_ready, b + 2)
                turn_a(b - 1)
                for j in range(4, UPU):
                    up_unit(j, q0 + j, (b, j))
                pe.wait_ge(sel_dn_ready, b)
                pe.wait_ge(y_ready, b)
                bias(4, 2, sel_dn, 2 * FF, dn_bias_done)
                pe.wait_ge(aT_ready, 2 * b)
                for j in range(DNU):
                    down_unit(j, q0 + UPU + j, (b, UPU + j))
                    if j == 1:
                        turn_x(b + 1)
            q0 = UPB * nb
            pe.wait_ge(xT_ready, 2 * nb + 2)
            turn_a(nb - 1)
            pe.wait_ge(sel_dn_ready, nb)
            pe.wait_ge(y_ready, nb)
            bias(4, 2, sel_dn, 2 * FF, dn_bias_done)
            pe.wait_ge(aT_ready, 2 * nb)
            for j in range(DNU):
                down_unit(j, q0 + j, (nb, j, True))



_INS = ["x_prompt", "x_sample", "state_gla", "cache_swa_k", "cache_swa_v", "meta_tokens", "rel_bias_table", "g_mix",
        "w_in", "w_a_up", "b_a", "g_gla_out", "g_swa_out", "attn_sinks", "w_out", "g_ffn", "w_router", "b_router",
        "w_up", "b_up", "w_down", "b_down", "g_final"]
_OUTS = [(1, SEQ, D), (NS, 1, D), (1, 1, GH, DK, DV), (1, 1, WIN, KVH, HD), (1, 1, WIN, KVH, HD), (1, NS, GH, DK, DV),
         (1, NS, WIN, KVH, HD), (1, NS, WIN, KVH, HD)]


def _bucket(dist):
    exact = BUCKETS // 2
    if dist < exact:
        return dist
    return min(exact + int(math.log(dist / exact) / math.log(WIN / exact) * (BUCKETS - exact)), BUCKETS - 1)


def kernel(**inputs):
    import numpy as _np
    import concourse.bacc as _bacc
    from concourse import mybir as _mybir
    from concourse.bass_utils import run_bass_kernel_spmd as _run

    nc = _bacc.Bacc("TRN2", target_bir_lowering=False, num_devices=1)
    arrays, args = {}, []
    for name in _INS:
        a = _np.ascontiguousarray(inputs[name])
        arrays[f"in_{name}_dram"] = a
        args.append(nc.dram_tensor(f"in_{name}_dram", a.shape, _mybir.dt.from_np(a.dtype), kind="ExternalInput").ap())
    hot = _np.zeros((BUCKETS, WIN), _np.float32)
    for x in range(WIN):
        hot[_bucket(WIN - 1 - x), x] = 1.0
    arrays["in_bucket_dram"] = hot
    args.append(nc.dram_tensor("in_bucket_dram", hot.shape, F32, kind="ExternalInput").ap())
    for i, shape in enumerate(_OUTS):
        args.append(nc.dram_tensor(f"out_{i}_dram", shape, F32, kind="ExternalOutput").ap())
    moe_layer(nc, *args)
    r = _run(nc, [arrays], core_ids=[0])
    return tuple(r.results[0][f"out_{i}_dram"] for i in range(len(_OUTS)))
```
